# Optimizing a Trainium2 kernel written in Bass

```python
import math
import jax
import jax.numpy as jnp
from jax import lax
import numpy as np

D_MODEL = 2048
BATCH = 1
SEQ = 256
DEPTH = 1
DEC_BATCH = 8
DEC_SEQ = 8
PAST_LEN = 2048
PAGE_SIZE = 128

LRU_WIDTH = D_MODEL // 2
LRU_BLOCKS = 16
LRU_BLOCK = LRU_WIDTH // LRU_BLOCKS
LRU_C = 8.0
CONV_WIDTH = 4
DN_HEAD_DIM = 128
DN_HEADS = (D_MODEL // 2) // DN_HEAD_DIM
DN_DK = DN_HEAD_DIM
DN_DV = DN_HEAD_DIM
DN_QK = DN_HEADS * DN_DK
DN_VW = DN_HEADS * DN_DV
DN_CHUNK = 64
POOL_WIDTH = D_MODEL // 2
POOL_WINDOWS = (2, 4, 8, 16)
POOL_GROUPS = 4
POOL_GROUP = POOL_WIDTH // POOL_GROUPS
POOL_BUF = 15
D_FF = 4 * D_MODEL
EPS = 1e-6
IN_SPLITS = (LRU_WIDTH, LRU_WIDTH, DN_QK, DN_QK, DN_VW, DN_VW, DN_HEADS, DN_HEADS, POOL_WIDTH, D_MODEL, D_MODEL, D_MODEL)
D_IN = sum(IN_SPLITS)

kernel_name = 'hybrid_rglru_deltanet_pool_step'

def rmsnorm(x, gain):
    xf = x.astype(jnp.float32)
    y = xf * lax.rsqrt(jnp.mean(xf * xf, axis=-1, keepdims=True) + EPS)
    return (y * gain.astype(jnp.float32)).astype(x.dtype)

def split_cols(p):
    outs = []
    start = 0
    for w in IN_SPLITS:
        outs.append(p[..., start:start + w])
        start += w
    return outs

def causal_dwconv(x, buf, w, b=None):
    full = jnp.concatenate([buf.astype(x.dtype), x], axis=1)
    T = x.shape[1]
    y = sum(full[:, j:j + T] * w[j].astype(x.dtype) for j in range(CONV_WIDTH))
    if b is not None:
        y = y + b.astype(x.dtype)
    return y, full[:, T:]

def _lin_combine(c1, c2):
    a1, b1 = c1
    a2, b2 = c2
    return a1 * a2, a2 * b1 + b2

def rg_lru(x, w_a, b_a, w_x, b_x, lam, h0):
    B, T, _ = x.shape
    f32 = jnp.float32
    xf = x.astype(f32)
    xb = xf.reshape(B, T, LRU_BLOCKS, LRU_BLOCK)
    r = jax.nn.sigmoid(jnp.einsum('btnc,ncd->btnd', xb, w_a.astype(f32)).reshape(B, T, LRU_WIDTH) + b_a.astype(f32))
    i = jax.nn.sigmoid(jnp.einsum('btnc,ncd->btnd', xb, w_x.astype(f32)).reshape(B, T, LRU_WIDTH) + b_x.astype(f32))
    log_a = -LRU_C * r * jax.nn.softplus(-lam.astype(f32))
    a = jnp.exp(log_a)
    bterm = jnp.sqrt(-jnp.expm1(2.0 * log_a)) * (i * xf)
    bterm = bterm.at[:, 0].add(a[:, 0] * h0.astype(f32))
    _, h = lax.associative_scan(_lin_combine, (a, bterm), axis=1)
    return h, h[:, -1]

def l2norm(x):
    return x * lax.rsqrt(jnp.sum(x * x, axis=-1, keepdims=True) + EPS)

def gated_delta_rule(q, k, v, beta, g, s0):
    B, T, H, DK = q.shape
    DV = v.shape[-1]
    C = DN_CHUNK if T >= DN_CHUNK else T
    n = -(-T // C)
    pad = n * C - T

    def prep(a):
        a = jnp.pad(a, [(0, 0), (0, pad)] + [(0, 0)] * (a.ndim - 2))
        a = a.reshape((B, n, C) + a.shape[2:])
        return jnp.moveaxis(a, (1, 3), (0, 2))

    q, k, v, beta, g = prep(q), prep(k), prep(v), prep(beta), prep(g)
    gamma = jnp.cumsum(g, axis=-1)
    incl = jnp.tril(jnp.ones((C, C), dtype=bool))
    strict = jnp.tril(jnp.ones((C, C), dtype=bool), k=-1)
    decay = jnp.exp(jnp.where(incl, gamma[..., :, None] - gamma[..., None, :], -jnp.inf))
    kk = jnp.einsum('nbhik,nbhjk->nbhij', k, k)
    a_mat = jnp.eye(C, dtype=jnp.float32) + jnp.where(strict, beta[..., None] * decay * kk, 0.0)
    eg = jnp.exp(gamma)
    rhs = jnp.concatenate([beta[..., None] * v, (beta * eg)[..., None] * k], axis=-1)
    sol = lax.linalg.triangular_solve(a_mat, rhs, left_side=True, lower=True, unit_diagonal=True)
    u_c, wk_c = sol[..., :DV], sol[..., DV:]
    qk = jnp.einsum('nbhik,nbhjk->nbhij', q, k) * decay
    qg = q * eg[..., None]
    kd = k * jnp.exp(gamma[..., -1:] - gamma)[..., None]
    g_last = jnp.exp(gamma[..., -1])

    def step(s, inp):
        qg_c, kd_c, uc, wkc, qk_c, gl_c = inp
        w = uc - jnp.einsum('bhck,bhkv->bhcv', wkc, s)
        o = jnp.einsum('bhck,bhkv->bhcv', qg_c, s) + jnp.einsum('bhij,bhjv->bhiv', qk_c, w)
        s = gl_c[..., None, None] * s + jnp.einsum('bhck,bhcv->bhkv', kd_c, w)
        return s, o

    s_last, o = lax.scan(step, s0, (qg, kd, u_c, wk_c, qk, g_last))
    o = jnp.moveaxis(o, (0, 2), (1, 3)).reshape(B, n * C, H, DV)[:, :T]
    return o, s_last

def multiscale_pool(u, buf, past_len, w_pool, scale):
    B, T, _ = u.shape
    f32 = jnp.float32
    P = POOL_BUF
    full = jnp.concatenate([buf.astype(f32), u.astype(f32)], axis=1)
    cs = jnp.concatenate([jnp.zeros((B, 1, POOL_WIDTH), f32), jnp.cumsum(full, axis=1)], axis=1)
    pos = jnp.arange(T) + 1 + past_len
    means = []
    for gi, w in enumerate(POOL_WINDOWS):
        c0 = gi * POOL_GROUP
        c1 = c0 + POOL_GROUP
        s = cs[:, P + 1:P + 1 + T, c0:c1] - cs[:, P + 1 - w:P + 1 - w + T, c0:c1]
        cnt = jnp.minimum(pos, w).astype(f32)
        means.append(s / cnt[None, :, None])
    pooled = jnp.concatenate(means, axis=-1)
    d = (pooled - full[:, P:]).reshape(B, T, POOL_GROUPS, POOL_GROUP)
    y = jnp.einsum('btgc,gcd->btgd', d, w_pool.astype(f32)).reshape(B, T, POOL_WIDTH) * scale.astype(f32)
    return y.astype(u.dtype), full[:, T:].astype(u.dtype)

def layer(x, past_len, h0, lru_buf, s0, dn_buf, pool_buf,
          norm_mix, w_in, lru_conv_w, lru_conv_b, lru_gate_a_w, lru_gate_a_b, lru_gate_x_w, lru_gate_x_b,
          lru_lambda, dn_conv_w, dn_a_log, dn_dt_bias, dn_norm_w, pool_w, pool_scale,
          w_br_lru, w_br_dn, w_br_pool, w_out, norm_mlp, w_up, w_down):
    B, T, _ = x.shape
    f32 = jnp.float32
    xn = rmsnorm(x, norm_mix)
    xl, gl, q, k, v, z, b_raw, a_raw, u_pool, g_lru, g_dn, g_pool = split_cols(xn @ w_in)

    xl, new_lru_buf = causal_dwconv(xl, lru_buf, lru_conv_w, lru_conv_b)
    h, h_last = rg_lru(xl, lru_gate_a_w, lru_gate_a_b, lru_gate_x_w, lru_gate_x_b, lru_lambda, h0)
    o_lru = (h * jax.nn.gelu(gl.astype(f32))).astype(x.dtype)

    qkv, new_dn_buf = causal_dwconv(jnp.concatenate([q, k, v], axis=-1), dn_buf, dn_conv_w)
    qkv = jax.nn.silu(qkv.astype(f32))
    qh = l2norm(qkv[..., :DN_QK].reshape(B, T, DN_HEADS, DN_DK)) * (DN_DK ** -0.5)
    kh = l2norm(qkv[..., DN_QK:2 * DN_QK].reshape(B, T, DN_HEADS, DN_DK))
    vh = qkv[..., 2 * DN_QK:].reshape(B, T, DN_HEADS, DN_DV)
    beta = jax.nn.sigmoid(b_raw.astype(f32))
    g = -jnp.exp(dn_a_log.astype(f32)) * jax.nn.softplus(a_raw.astype(f32) + dn_dt_bias.astype(f32))
    o, s_last = gated_delta_rule(qh, kh, vh, beta, g, s0.astype(f32))
    o = o * lax.rsqrt(jnp.mean(o * o, axis=-1, keepdims=True) + EPS) * dn_norm_w.astype(f32)
    o = o * jax.nn.silu(z.astype(f32).reshape(B, T, DN_HEADS, DN_DV))
    o_dn = o.reshape(B, T, DN_VW).astype(x.dtype)

    o_pool, new_pool_buf = multiscale_pool(u_pool, pool_buf, past_len, pool_w, pool_scale)

    merged = (jax.nn.sigmoid(g_lru) * (o_lru @ w_br_lru)
              + jax.nn.sigmoid(g_dn) * (o_dn @ w_br_dn)
              + jax.nn.sigmoid(g_pool) * (o_pool @ w_br_pool))
    x = x + merged @ w_out

    hm = jnp.square(jax.nn.relu(rmsnorm(x, norm_mlp) @ w_up))
    x = x + hm @ w_down
    return x, (h_last, new_lru_buf, s_last, new_dn_buf, new_pool_buf)

def setup_inputs(seed: int = 0) -> dict:
    key = jax.random.key(seed)
    ks = iter(jax.random.split(key, 40))
    f32 = jnp.float32
    L = DEPTH
    dn_conv_ch = 2 * DN_QK + DN_VW

    def nrm(shape, scale):
        return jax.random.normal(next(ks), shape, f32) * scale

    x_prompt = nrm((BATCH, SEQ, D_MODEL), 1.0)
    x_sample = nrm((DEC_BATCH, DEC_SEQ, D_MODEL), 1.0)
    state_lru_h = nrm((L, DEC_BATCH, LRU_WIDTH), 0.5)
    state_lru_conv = nrm((L, DEC_BATCH, CONV_WIDTH - 1, LRU_WIDTH), 1.0)
    state_dn_s = nrm((L, DEC_BATCH, DN_HEADS, DN_DK, DN_DV), 0.05)
    state_dn_conv = nrm((L, DEC_BATCH, CONV_WIDTH - 1, dn_conv_ch), 1.0)
    state_pool = nrm((L, DEC_BATCH, POOL_BUF, POOL_WIDTH), 1.0)
    norm_mix = 1.0 + nrm((L, D_MODEL), 0.02)
    w_in = nrm((L, D_MODEL, D_IN), D_MODEL ** -0.5)
    lru_conv_w = nrm((L, CONV_WIDTH, LRU_WIDTH), CONV_WIDTH ** -0.5)
    lru_conv_b = nrm((L, LRU_WIDTH), 0.02)
    lru_gate_a_w = nrm((L, LRU_BLOCKS, LRU_BLOCK, LRU_BLOCK), LRU_BLOCK ** -0.5)
    lru_gate_a_b = nrm((L, LRU_WIDTH), 0.02)
    lru_gate_x_w = nrm((L, LRU_BLOCKS, LRU_BLOCK, LRU_BLOCK), LRU_BLOCK ** -0.5)
    lru_gate_x_b = nrm((L, LRU_WIDTH), 0.02)
    a0 = jax.random.uniform(next(ks), (L, LRU_WIDTH), f32, 0.9, 0.999)
    lru_lambda = jnp.log(a0) - jnp.log1p(-a0)
    dn_conv_w = nrm((L, CONV_WIDTH, dn_conv_ch), CONV_WIDTH ** -0.5)
    dn_a_log = jnp.log(jax.random.uniform(next(ks), (L, DN_HEADS), f32, 1.0, 16.0))
    dt = jnp.exp(jax.random.uniform(next(ks), (L, DN_HEADS), f32, math.log(1e-3), math.log(1e-1)))
    dn_dt_bias = dt + jnp.log(-jnp.expm1(-dt))
    dn_norm_w = 1.0 + nrm((L, DN_DV), 0.02)
    pool_w = nrm((L, POOL_GROUPS, POOL_GROUP, POOL_GROUP), POOL_GROUP ** -0.5)
    pool_scale = 1.0 + nrm((L, POOL_WIDTH), 0.02)
    w_br_lru = nrm((L, LRU_WIDTH, D_MODEL), LRU_WIDTH ** -0.5)
    w_br_dn = nrm((L, DN_VW, D_MODEL), DN_VW ** -0.5)
    w_br_pool = nrm((L, POOL_WIDTH, D_MODEL), POOL_WIDTH ** -0.5)
    w_out = nrm((L, D_MODEL, D_MODEL), D_MODEL ** -0.5)
    norm_mlp = 1.0 + nrm((L, D_MODEL), 0.02)
    w_up = nrm((L, D_MODEL, D_FF), D_MODEL ** -0.5)
    w_down = nrm((L, D_FF, D_MODEL), D_FF ** -0.5)
    norm_final = 1.0 + nrm((D_MODEL,), 0.02)
    return {'x_prompt': x_prompt, 'x_sample': x_sample,
            'state_lru_h': state_lru_h, 'state_lru_conv': state_lru_conv, 'state_dn_s': state_dn_s,
            'state_dn_conv': state_dn_conv, 'state_pool': state_pool,
            'norm_mix': norm_mix, 'w_in': w_in, 'lru_conv_w': lru_conv_w, 'lru_conv_b': lru_conv_b,
            'lru_gate_a_w': lru_gate_a_w, 'lru_gate_a_b': lru_gate_a_b, 'lru_gate_x_w': lru_gate_x_w,
            'lru_gate_x_b': lru_gate_x_b, 'lru_lambda': lru_lambda, 'dn_conv_w': dn_conv_w,
            'dn_a_log': dn_a_log, 'dn_dt_bias': dn_dt_bias, 'dn_norm_w': dn_norm_w, 'pool_w': pool_w,
            'pool_scale': pool_scale, 'w_br_lru': w_br_lru, 'w_br_dn': w_br_dn, 'w_br_pool': w_br_pool,
            'w_out': w_out, 'norm_mlp': norm_mlp, 'w_up': w_up, 'w_down': w_down, 'norm_final': norm_final}

def reference(x_prompt, x_sample, state_lru_h, state_lru_conv, state_dn_s, state_dn_conv, state_pool,
              norm_mix, w_in, lru_conv_w, lru_conv_b, lru_gate_a_w, lru_gate_a_b, lru_gate_x_w, lru_gate_x_b,
              lru_lambda, dn_conv_w, dn_a_log, dn_dt_bias, dn_norm_w, pool_w, pool_scale,
              w_br_lru, w_br_dn, w_br_pool, w_out, norm_mlp, w_up, w_down, norm_final):
    f32 = jnp.float32
    bp = x_prompt.shape[0]
    dt = x_prompt.dtype
    p_h0 = jnp.zeros((bp, LRU_WIDTH), f32)
    p_lru_buf = jnp.zeros((bp, CONV_WIDTH - 1, LRU_WIDTH), dt)
    p_s0 = jnp.zeros((bp, DN_HEADS, DN_DK, DN_DV), f32)
    p_dn_buf = jnp.zeros((bp, CONV_WIDTH - 1, 2 * DN_QK + DN_VW), dt)
    p_pool_buf = jnp.zeros((bp, POOL_BUF, POOL_WIDTH), dt)
    xp, xs = x_prompt, x_sample
    p_st, s_st = [], []
    for l in range(DEPTH):
        params = (norm_mix[l], w_in[l], lru_conv_w[l], lru_conv_b[l], lru_gate_a_w[l], lru_gate_a_b[l],
                  lru_gate_x_w[l], lru_gate_x_b[l], lru_lambda[l], dn_conv_w[l], dn_a_log[l], dn_dt_bias[l],
                  dn_norm_w[l], pool_w[l], pool_scale[l], w_br_lru[l], w_br_dn[l], w_br_pool[l], w_out[l],
                  norm_mlp[l], w_up[l], w_down[l])
        xp, st = layer(xp, 0, p_h0, p_lru_buf, p_s0, p_dn_buf, p_pool_buf, *params)
        p_st.append(st)
        xs, st = layer(xs, PAST_LEN, state_lru_h[l], state_lru_conv[l], state_dn_s[l], state_dn_conv[l],
                       state_pool[l], *params)
        s_st.append(st)
    y_prompt = rmsnorm(xp, norm_final)
    y_sample = rmsnorm(xs, norm_final)
    p_lru_h = jnp.stack([s[0] for s in p_st])
    p_lru_conv = jnp.stack([s[1] for s in p_st])
    p_dn_s = jnp.stack([s[2] for s in p_st])
    p_dn_conv = jnp.stack([s[3] for s in p_st])
    p_pool = jnp.stack([s[4] for s in p_st])
    s_lru_h = jnp.stack([s[0] for s in s_st])
    s_lru_conv = jnp.stack([s[1] for s in s_st])
    s_dn_s = jnp.stack([s[2] for s in s_st])
    s_dn_conv = jnp.stack([s[3] for s in s_st])
    s_pool = jnp.stack([s[4] for s in s_st])
    return (y_prompt, y_sample, p_lru_h, p_lru_conv, p_dn_s, p_dn_conv, p_pool,
            s_lru_h, s_lru_conv, s_dn_s, s_dn_conv, s_pool)


_drawn_inputs = setup_inputs


def setup_inputs(seed=0):
    import zlib

    import numpy as np

    out = dict(_drawn_inputs(seed))
    spreads = {}
    factors = {'lru_gate_a_b': 8.0,
     'lru_gate_x_b': 7.871,
     'dn_norm_w': 8.0,
     'pool_scale': 6.241,
     'norm_mlp': 3.462,
     'norm_final': 2.848}
    for name, (base, spread) in spreads.items():
        noise = np.random.default_rng([zlib.crc32(name.encode()), seed]).standard_normal(out[name].shape)
        drawn = base * np.exp(spread * noise) if base else spread * noise
        out[name] = jnp.asarray(drawn.astype(out[name].dtype))
    for name, factor in factors.items():
        out[name] = (out[name] * factor).astype(out[name].dtype)
    return out
```

```python
from contextlib import ExitStack

import numpy as np
import concourse.bass as bass
from concourse import mybir

ALU = mybir.AluOpType
ACT = mybir.ActivationFunctionType
F32 = mybir.dt.float32
F32R = mybir.dt.float32r

P = 128
D = 2048
NP, DB, DT = 256, 8, 8
NS = DB * DT
N = NP + NS
W = D // 2
FF = 4 * D
KD, KW = D // P, W // P
HEADS = W // P
CW = 4
PB = 15
GROUPS, GW_ = 4, 256
EPS = 1e-6
XL0, GL0, Q0, BA0 = 0, W, 2 * W, 6 * W
Z0 = 5 * W
U0 = 6 * W + 2 * HEADS
G0 = {"lru": U0 + W, "dn": U0 + W + D, "pool": U0 + W + 2 * D}
BACK = {"lru": D, "dn": D + W, "pool": D + 2 * W}
CT = 32

C_MIX, C_MLP, C_FIN, C_CW = 0, KD, 2 * KD, 3 * KD
C_CB = C_CW + CT * CW
C_GA, C_GX, C_LAM, C_PS = C_CB + KW, C_CB + 2 * KW, C_CB + 3 * KW, C_CB + 4 * KW
C_DNW = C_CB + 5 * KW
C_ALOG, C_DTB = C_DNW + 1, C_DNW + 2
NPAR = C_DNW + 3

RING = 4
TILE = 4 * 256
QKV_N, QKV_T = 2, 0
LRU_N, LRU_T = QKV_N + 6 * 8, QKV_T + 6 * 4
GPL_N, GPL_T = LRU_N + 4 * 8, LRU_T + 4 * 4
POOL_N, POOL_T = GPL_N + 4 * 12, GPL_T + 4 * 8
GPP_N, GPP_T = POOL_N + 16, POOL_T + 8
Z_N, Z_T = GPP_N + 4 * 12, GPP_T + 4 * 8
GPD_N, GPD_T = Z_N + 16, Z_T + 8
OUT_N, OUT_T = GPD_N + 4 * 12, GPD_T + 4 * 8
MLP_N, MLP_T = OUT_N + 4 * 8, OUT_T + 4 * 4


class Chain:

    def __init__(self, eng, sem):
        self.eng, self.sem, self.n, self.loop = eng, sem, 0, None

    def link(self, ins):
        ins.then_inc(self.sem, 1)
        self.n += 1
        if self.loop is None:
            self.eng.wait_ge(self.sem, self.n)
        else:
            it, start, first, per = self.loop
            self.eng.wait_ge(self.sem, it * per + (self.n - first * per))

    def enter(self, it, first, per):
        assert self.loop is None
        self.loop = (it, self.n, first, per)

    def leave(self, times, name):
        _, start, _, per = self.loop
        assert self.n - start == per, (name, self.n - start)
        self.n, self.loop = start + times * per, None


def cols(t, index, width, lo=0, n=None, rows=P):
    n = width if n is None else n
    if isinstance(index, int):
        return t[0:rows, index * width + lo:index * width + lo + n]
    return t[0:rows, bass.ds(index * width + lo, n)]


def build(nc, A):
    with ExitStack() as ctx:
        place = [(nc.sbuf_base + 31) // 32 * 32]

        def sb(name, n, dt=F32):
            t = nc.alloc_sbuf_tensor_at(name, [P, n], dt, offset=place[0])
            place[0] += (4 * n + 31) // 32 * 32
            return t

        RAW, HI, LO = sb("raw", RING * TILE), sb("hi", RING * TILE, F32R), sb("lo", RING * TILE, F32R)
        XH, XL = sb("x_hi", KD * N, F32R), sb("x_lo", KD * N, F32R)
        OH, OL = sb("o_hi", KW * N, F32R), sb("o_lo", KW * N, F32R)
        MG = sb("merged", KD * N)
        at_qkv = place[0]
        QKV = sb("qkv", 24 * N)
        SCR = sb("scratch", 24 * N)
        at_end = place[0]
        MH = nc.alloc_sbuf_tensor_at("merged_hi", [P, KD * N], F32R, offset=at_qkv + 4 * KD * N)
        ML = nc.alloc_sbuf_tensor_at("merged_lo", [P, KD * N], F32R, offset=at_qkv + 8 * KD * N)
        assert at_qkv + 12 * KD * N == at_end
        X2 = QKV[:, 0:KD * N]
        V0 = 16 * N
        PRM = sb("params", NPAR)
        R = sb("rms_scale", N)
        GS = sb("gate", 2 * N)
        RN, BG = sb("qk_scale_rows", N), sb("beta_gamma_rows", N)
        RS, SELS = sb("rows_split", 2 * N, F32R), sb("row_pickers", 2 * P, F32R)
        COL = sb("token_columns", 3 * 56)
        MASKI = sb("mask_incl", N)
        LM = sb("level_masks", 6 * P)
        M1T = sb("mask_first_t", P)
        ident, ones = sb("ident", P), sb("ones", P)
        EONE = sb("one_column", 32)
        ID2 = sb("ident_pairs", 8)
        BM = sb("batch_mask", DB)
        LH0, LHO = sb("lru_h0", KW * DB), sb("lru_h_out", KW * (DB + 1))
        NSP = sb("lru_rate", KW)
        RC = sb("pool_recip", GROUPS * 16)
        F16 = sb("pool_first", 32)
        SMALL = sb("small", 4)
        assert place[0] <= nc.sbuf_usable_end, place[0]

        def scr(lo, n, rows=P):
            return SCR[0:rows, lo:lo + n]

        CI, CO, PAD = scr(0, CT * 24), scr(768, CT * 27), [scr(1632, 347), scr(1984, 347)]
        CV, TR, TI, TH, G2, GL, AA = (scr(2336 + 2 * N * i, 2 * N) for i in range(7))
        GWT = scr(2336 + 14 * N, 4 * P)
        SEG = scr(2336 + 14 * N + 4 * P, N, 16)
        ROW = [SCR[0:16, 2976 + N * i:2976 + N * (i + 1)] for i in (0, 1, 2, 3, 6, 7, 8, 9, 10, 11)]
        SQ8, SQA = MG[:, 0:8 * N], MG[:, 0:2 * N]
        HR = nc.alloc_sbuf_tensor_at("head_rows", [P, 2 * N], F32R, offset=at_qkv + 4 * 24 * N)
        RM = [HR[0:48, 0:N], HR[0:48, N:2 * N]]
        WX = scr(2 * N, 8 * P, NS)
        VT, XX, YY = scr(2 * N, N), scr(3 * N, N), scr(4 * N, N)
        o = 5 * N + 64
        XT, KT, QT, KB, EG, COMB, DTM, LT, QKD = (
            scr(o, N), scr(o + N, N), scr(o + 2 * N, N), scr(o + 3 * N, N), scr(o + 4 * N, N),
            scr(o + 5 * N, 2 * N), scr(o + 7 * N, N), scr(o + 8 * N, N), scr(o + 9 * N, N))
        o += 10 * N
        VB, KBG, KDC = scr(o, 3 * P), scr(o + 3 * P, 3 * P), scr(o + 6 * P, 3 * P)
        W0, U12, S1, WS = scr(o + 9 * P, P), scr(o + 10 * P, 2 * P), scr(o + 12 * P, P), scr(o + 13 * P, P)
        SS = scr(o + 14 * P, DB * P)
        assert o + 22 * P == 24 * N
        UP = scr(0, 910)
        SA, SB_ = scr(910, 910), scr(1820, 910)
        DD = scr(2730, 2 * N)
        PW = scr(3370, GROUPS * 2 * GW_)
        PI, PO = scr(5418, KW * DB * PB), scr(6378, KW * (DB + 1) * PB)
        ZT, O1 = scr(0, 2 * N), scr(2 * N, 2 * N)
        RO = scr(4 * N, N, 16)
        ZRM = [scr(5 * N, N, 16), scr(6 * N, N, 16)]
        OSQ = scr(7 * N, 8 * N)
        RT = [scr(15 * N, N), scr(16 * N, N)]
        HF = scr(0, 2 * N)
        T0, T1, T2 = RT[0], RT[1], scr(17 * N, N)

        MB = [ctx.enter_context(nc.psum_tensor(f"main{i}", [P, 512], F32)) for i in range(4)]
        AX = [ctx.enter_context(nc.psum_tensor(f"aux{i}", [P, 512], F32)) for i in range(4)]

        def sem(name):
            return ctx.enter_context(nc.semaphore(name))

        raw_full = [sem(f"raw_full{i}") for i in range(RING)]
        hi_ready = sem("hi_ready")
        lo_ready, tile_used, evacuated = sem("lo_ready"), sem("tile_used"), sem("evacuated")
        (const_loaded, conv_in_loaded, ones_ready, masks_ready, xhi_ready, xlo_ready, sq_used, var_ready, sqrt_ready) = map(sem, (
            "const_loaded", "conv_in_loaded", "ones_ready", "masks_ready", "xhi_ready", "xlo_ready", "sq_used", "var_ready",
            "sqrt_ready"))
        x_loaded = [sem(f"x_loaded{i}") for i in range(4)]
        prefix_ready, tail_copied, conv_ready, th_ready, qkv_ready = map(sem, (
            "prefix_ready", "tail_copied", "conv_ready", "th_ready", "qkv_ready"))
        (row_a, row_b, row_c, row_d, row_e, row_f, row_g, row_psum, row_cols, row_beg, qk_sq) = map(sem, (
            "row_abs", "row_exp", "row_one_plus", "row_ln", "row_decay", "row_decay_exp", "row_gamma", "row_psum",
            "row_cols", "row_exp_cols", "qk_sq"))
        (gw_loaded, gates_psum, gate_tanh, la_ready, a_ready, m_ready, root_ready, h_ready, lho_copied,
         gsq_ready, gin_ready, gth_ready) = map(sem, (
            "gw_loaded", "gates_psum", "gate_tanh", "log_a_ready", "a_ready", "one_minus_a2", "root_ready",
            "h_ready", "lho_copied", "gelu_sq", "gelu_in", "gelu_tanh"))
        of_ready, ohi_ready, o_ready = sem("of_ready"), sem("ohi_ready"), sem("o_ready")
        gate_ready, merged_ready, mhi_ready, mlo_ready = map(sem, (
            "gate_ready", "merged_ready", "merged_hi_ready", "merged_lo_ready"))
        (rm_ready, bc_psum, dt_ready, dt_exp, dtm_ready, qg_ready, khat_ready, vt_ready, tok_psum, tok_scaled,
         lt_ready, xt_psum, x_ready, y_psum, y_ready, z_psum, uw_psum, w0_ready, s1_psum, s1_ready, ws_ready,
         w1_psum, w_ready, fin_psum, dn_done, ss_loaded, ss_stored) = map(sem, (
            "dn_rows", "dn_bcast_psum", "dn_decay_in", "dn_decay_exp", "dn_decay_masked", "dn_qg", "dn_khat",
            "dn_v_copied", "dn_tok_psum", "dn_tok_scaled", "dn_lt", "dn_xt_psum", "dn_x", "dn_y_psum", "dn_y",
            "dn_z_psum", "dn_uw_psum", "dn_w0", "dn_s1_psum", "dn_s1", "dn_ws", "dn_w1_psum", "dn_w", "dn_fin_psum",
            "dn_done", "dn_state_loaded", "dn_state_stored"))
        pool_loaded, pfx_ready, ptail_copied, d_ready, py_psum = map(sem, (
            "pool_loaded", "pool_prefix", "pool_tail", "pool_d", "pool_psum"))
        osq_ready, o_ss_psum, ro_ready, zm_ready, zb_psum, zr_tanh = map(sem, (
            "o_sq", "o_ss_psum", "o_scale_rows", "z_rows", "z_bcast", "z_tanh"))
        x2_loaded, sq2_ready, sq2_used, xh2_ready, xg2_ready = map(sem, (
            "residual_loaded", "sq2_ready", "sq2_used", "xh2_ready", "xg2_ready"))
        hf_ready, hm_ready, out_ready = map(sem, ("relu2_hi", "relu2_lo", "out_ready"))
        out_stored, y_stored = sem("out_stored"), sem("y_stored")
        dve_step, act_step, pool_step = sem("dve_step"), sem("act_step"), sem("pool_step")

        block = ctx.enter_context(nc.Block())

        @block.sync
        def _(sp):
            for i in range(4):
                sp.dma_start(MG[:, 4 * i * N:4 * (i + 1) * N], A["x"][:, 4 * i * N:4 * (i + 1) * N]) \
                    .then_inc(x_loaded[i], 16)
                if i == 0:
                    for j in range(2):
                        sp.dma_start(RAW[:, j * TILE:(j + 1) * TILE].rearrange("p (b c) -> p b c", b=8),
                                     A["w_in"][j * 1024:(j + 1) * 1024, BA0:BA0 + P]
                                     .rearrange("(b p) c -> p b c", p=P)).then_inc(raw_full[j], 16)

            def load(n0, per, it, j, w, row, col):
                slot = (n0 + j) % RING
                if not isinstance(it, int) or n0 + j + it * per >= RING:
                    sp.wait_ge(lo_ready, it * per + (n0 + j + 1))
                rows = w[row:row + 512] if isinstance(row, int) else w[bass.ds(row, 512)]
                src = rows[:, col:col + 256] if isinstance(col, int) else rows[:, bass.ds(col, 256)]
                sp.dma_start(RAW[:, slot * TILE:(slot + 1) * TILE].rearrange("p (b c) -> p b c", b=4),
                             src.rearrange("(b p) c -> p b c", p=P)).then_inc(raw_full[slot], 16)

            def qkv(it):
                for j in range(8):
                    load(QKV_N, 8, it, j, A["w_in"], j % 4 * 512, it * 512 + (Q0 + j // 4 * 256))

            def lru(it):
                for j in range(8):
                    load(LRU_N, 8, it, j, A["w_in"], j % 4 * 512, it * 256 + (XL0, GL0)[j // 4])

            def gated(it, n0, name):
                for s in range(2):
                    for j in range(4):
                        load(n0, 12, it, 6 * s + j, A["w_in"], j * 512, it * 512 + (G0[name] + s * 256))
                    for j in range(2):
                        load(n0, 12, it, 6 * s + 4 + j, A["w_back"], BACK[name] + j * 512, it * 512 + s * 256)

            qkv(0)
            with sp.Fori(1, 6) as it:
                qkv(it)
            with sp.Fori(0, 4) as it:
                lru(it)
            with sp.Fori(0, 4) as it:
                gated(it, GPL_N, "lru")
            for j in range(16):
                load(POOL_N, 16, 0, j, A["w_in"], j % 4 * 512, U0 + j // 4 * 256)
            with sp.Fori(0, 4) as it:
                gated(it, GPP_N, "pool")
            for j in range(16):
                load(Z_N, 16, 0, j, A["w_in"], j % 4 * 512, Z0 + j // 4 * 256)
            with sp.Fori(0, 4) as it:
                gated(it, GPD_N, "dn")
            with sp.Fori(0, 4) as it:
                for j in range(8):
                    load(OUT_N, 8, it, j, A["w_back"], j % 4 * 512, it * 512 + j // 4 * 256)
            with sp.Fori(0, 8) as it:
                for j in range(16):
                    load(MLP_N, 32, it, j, A["w_up"], j % 4 * 512, it * 1024 + j // 4 * 256)
                for j in range(16):
                    d = j // 4 * 2 + j % 2
                    load(MLP_N, 32, it, 16 + j, A["w_down"], it * 1024 + j // 2 % 2 * 512, d * 256)
            for i in range(4):
                sp.wait_ge(out_ready, 4 * (i + 1))
                sp.dma_start(A["y"][:, 4 * i * N:4 * (i + 1) * N], MG[:, 4 * i * N:4 * (i + 1) * N]) \
                    .then_inc(y_stored, 16)
            sp.wait_ge(y_stored, 64)

        @block.gpsimd
        def _(pool):
            ch = Chain(pool, pool_step)
            pool.dma_start(CI, A["conv_in"]).then_inc(conv_in_loaded, 16)
            pool.dma_start(GWT, A["gates"][:, 0:4 * P]).then_inc(gw_loaded, 16)

            def select(t, pattern, base, mult, op=ALU.is_ge, fill=0.0):
                ch.link(pool.affine_select(out=t, in_=t, compare_op=op, fill=fill, base=base,
                                           pattern=pattern, channel_multiplier=mult))

            pool.memset(ones[:], 1.0).then_inc(ones_ready, 1)
            pool.memset(EONE[:], 0.0)
            pool.memset(PAD[0][:, 0:CW - 1], 0.0)
            pool.memset(PAD[1][:, 0:CW - 1], 0.0)
            pool.memset(ident[:], 0.0)
            pool.memset(MASKI[:], 1.0)
            pool.memset(LM[:], 1.0)
            pool.memset(M1T[:], 1.0)
            pool.memset(BM[:], 1.0)
            pool.memset(RS[:].bitcast(F32), 0.0)
            pool.memset(SELS[:].bitcast(F32), 0.0)
            pool.memset(ID2[:], 0.0)
            pool.memset(SEG, 1.0)
            pool.memset(SMALL[:, 0:2], 1.0)
            for g in range(GROUPS):
                pool.memset(RC[:, 16 * g:16 * (g + 1)], 1.0 / (2 << g))
            ch.link(pool.memset(F16[:], 0.0))
            pool.memset(EONE[:, 15:16], 1.0)
            ch.link(pool.memset(SELS[0:8, 0:P].bitcast(F32), 1.0))
            ch.link(pool.memset(SELS[32:40, 0:P].bitcast(F32), 1.0))
            for g in range(GROUPS):
                for t in range((2 << g) - 1):
                    pool.memset(RC[:, 16 * g + t:16 * g + t + 1], 1.0 / (t + 1))
            pool.memset(SEG[:, 0:NP:P], 0.0)
            pool.memset(SEG[:, NP:N:DT], 0.0)
            pool.memset(SMALL[0:HEADS, 0:1], float(P) ** -0.5)
            select(ident[:], [[-1, P]], 0, 1, ALU.not_equal, 1.0)
            select(SMALL[:, 1:2], [[0, 1]], -HEADS, 1)
            for c in range(2):
                select(MASKI[:, c * P:(c + 1) * P], [[1, P]], 0, -1)
            select(MASKI[:, NP:N], [[1, NS]], 0, -1)
            select(MASKI[:, NP:N], [[-DT, DB], [0, DT]], 0, 1)
            select(MASKI[:, NP:N], [[DT, DB], [0, DT]], DT - 1, -1)
            select(BM[:], [[-DT, DB]], 0, 1)
            select(BM[:], [[DT, DB]], DT - 1, -1)
            for level in range(6):
                s = 2 << level
                m = LM[:, level * P:(level + 1) * P]
                nb = P // (2 * s)
                select(m, [[-2 * s, nb], [0, 2 * s]], -s, 1)
                select(m, [[2 * s, nb], [0, 2 * s]], 2 * s - 1, -1)
                select(m, [[0, nb], [-1, 2 * s]], s - 1, 0)
            select(M1T[:], [[-2, P // 2], [0, 2]], 0, 1)
            select(M1T[:], [[2, P // 2], [0, 2]], 0, -1)
            select(M1T[:], [[0, P // 2], [1, 2]], -1, 0)
            ch.link(pool.tensor_scalar(SMALL[:, 2:3], SMALL[:, 1:2], -1.0, 1.0, ALU.mult, ALU.add))
            for r in (0, 32):
                ins = pool.tensor_scalar(SELS[r:r + 16, P:2 * P], SELS[r:r + 16, 0:P].bitcast(F32), -1.0, 1.0,
                                         ALU.mult, ALU.add)
                ch.link(ins)
                ins = pool.tensor_tensor(ID2[r:r + 16, :], ident[r:r + 16, r:r + 8], ident[r:r + 16, r + 8:r + 16],
                                         ALU.add)
                if r == 0:
                    ch.link(ins)
            ins.then_inc(masks_ready, 1)
            pool.wait_ge(masks_ready, 1)
            pool.wait_ge(conv_in_loaded, 16)

            def history(strip, strips_done, ct, evac):
                if strips_done is not None:
                    pool.wait_ge(conv_ready, strips_done)
                    pool.wait_ge(tail_copied, strips_done)
                for m in range(2):
                    ins = pool.tensor_copy(
                        PAD[m][:, NP + 3:347].rearrange("p (b t) -> p b t", b=DB)[:, :, 0:CW - 1],
                        cols(CI, ct, 24, 24 * m, 24).rearrange("p (b t) -> p b t", b=DB))
                ins.then_inc(prefix_ready, 1)
                pool.wait_ge(evacuated, evac)
                for m in range(2):
                    pool.tensor_copy(cols(CO, ct, 27, 27 * m, 3), PAD[m][:, NP:NP + 3])
                    ins = pool.tensor_copy(
                        cols(CO, ct, 27, 27 * m + 3, 24).rearrange("p (b t) -> p b t", b=DB),
                        PAD[m][:, NP + 3:347].rearrange("p (b t) -> p b t", b=DB)[:, :, DT:DT + 3])
                ins.then_inc(tail_copied, 1)

            history(0, None, 0, 2 + RING)
            with pool.Fori(1, 12) as s:
                history(s, s, s * 2, s * 2 + (2 + RING))

            def lru(it):
                history(it + 12, it + 12, it * 2 + 24, it * 4 + (LRU_T + 2 + RING))
                pool.wait_ge(h_ready, it + 1)
                for m in range(2):
                    pool.tensor_copy(cols(LHO, it, 18, 9 * m, 1), TR[:, m * N + NP - 1:m * N + NP])
                    ins = pool.tensor_copy(cols(LHO, it, 18, 9 * m + 1, 8),
                                           TR[:, m * N + NP + DT - 1:(m + 1) * N:DT])
                ins.then_inc(lho_copied, 1)

            def gate_weights(it):
                pool.wait_ge(gates_psum, it)
                pool.dma_start(GWT, cols(A["gates"], it, 4 * P)).then_inc(gw_loaded, 16)

            lru(0)
            for it in range(1, 4):
                gate_weights(it)
                lru(it)
            pool.wait_ge(tail_copied, 16)
            pool.wait_ge(lho_copied, 4)
            pool.dma_start(A["conv_out"], CO).then_inc(out_stored, 16)
            pool.dma_start(A["lru_out"], LHO[:]).then_inc(out_stored, 16)
            pool.wait_ge(out_stored, 32)
            pool.wait_ge(o_ready, 4)

            def rows(h):
                if h:
                    pool.wait_ge(bc_psum, h)
                for i in range(2):
                    ins = pool.tensor_scalar(RM[i], RS[0:48, i * N:(i + 1) * N].bitcast(F32), ID2[0:48, h:h + 1],
                                             None, ALU.mult)
                ins.then_inc(rm_ready, 1)

            def head(h, following):
                pool.dma_start(SS.rearrange("p (b v) -> p b v", b=DB), A["s_in"][:, h].rearrange("b k v -> k b v")) \
                    .then_inc(ss_loaded, 16)
                pool.wait_ge(dt_exp, h + 1)
                pool.tensor_tensor(DTM, DTM, MASKI[:], ALU.mult).then_inc(dtm_ready, 1)
                pool.wait_ge(khat_ready, h + 1)
                pool.wait_ge(vt_ready, h + 1)
                pool.tensor_tensor(COMB[:, N:2 * N], QT, EG, ALU.mult).then_inc(qg_ready, 1)
                if following:
                    rows(h + 1)
                pool.wait_ge(dn_done, h + 1)
                pool.dma_start(A["s_out"][:, h].rearrange("b k v -> k b v"),
                               SS.rearrange("p (b v) -> p b v", b=DB)).then_inc(ss_stored, 16)
                pool.dma_start(A["p_out"][h], S1).then_inc(ss_stored, 16)
                pool.wait_ge(ss_stored, h * 32 + 32)

            def half(h0):
                rows(h0)
                for h in range(h0, h0 + 3):
                    head(h, True)
                head(h0 + 3, False)

            pool.wait_ge(row_beg, 2)
            ch.link(pool.memset(DTM, 0.0))
            half(0)

            pool.dma_start(PI, A["pool_in"]).then_inc(pool_loaded, 16)
            pool.dma_start(PW, A["pool_w"]).then_inc(pool_loaded, 16)
            ups = UP.rearrange("p (m c) -> p m c", m=2)
            ch.link(pool.memset(ups[:, :, 0:PB], 0.0))
            pool.wait_ge(pool_loaded, 32)
            samples = [ups[:, m, PB + NP:455].rearrange("p (b t) -> p b t", b=DB) for m in range(2)]
            for g in range(GROUPS):
                if g:
                    pool.wait_ge(d_ready, g)
                    pool.wait_ge(ptail_copied, g)
                for m in range(2):
                    c = 2 * g + m
                    ins = pool.tensor_copy(samples[m][:, :, 0:PB],
                                           PI[:, c * 120:(c + 1) * 120].rearrange("p (b t) -> p b t", b=DB))
                ins.then_inc(pfx_ready, 1)
                pool.wait_ge(pfx_ready, g + 1)
                pool.wait_ge(evacuated, POOL_T + 2 * g + 2 + RING)
                for m in range(2):
                    c = 2 * g + m
                    pool.tensor_copy(PO[:, c * 135:c * 135 + PB], ups[:, m, NP:NP + PB])
                    ins = pool.tensor_copy(
                        PO[:, c * 135 + PB:(c + 1) * 135].rearrange("p (b t) -> p b t", b=DB),
                        samples[m][:, :, DT:DT + PB])
                ins.then_inc(ptail_copied, 1)
            pool.wait_ge(ptail_copied, GROUPS)
            pool.dma_start(A["pool_out"], PO).then_inc(out_stored, 16)
            pool.wait_ge(out_stored, 48)
            pool.wait_ge(o_ready, 8)
            ch.link(pool.memset(DTM, 0.0))
            half(4)

            pool.wait_ge(ro_ready, 1)
            for s in range(4):
                if s:
                    pool.wait_ge(zb_psum, s)
                for m in range(2):
                    h = 2 * s + m
                    ins = pool.tensor_scalar(ZRM[m], RO, ident[0:16, h:h + 1], None, ALU.mult)
                ins.then_inc(zm_ready, 1)
            pool.wait_ge(o_ready, 12)
            pool.dma_start(X2, A["x"]).then_inc(x2_loaded, 16)
            pool.wait_ge(mlo_ready, 8)
            for n in (*range(1, 8), *range(9, 16)):
                pool.wait_ge(sq2_ready, n)
                if n > 1:
                    pool.wait_ge(sq2_used, n - 1)
                if n in (1, 9):
                    pool.tensor_copy(SQA, GS[:]).then_inc(sq2_used, 1)
                else:
                    pool.tensor_tensor(SQA, SQA, GS[:], ALU.add).then_inc(sq2_used, 1)

        def joined(a, b):
            return {i: [*a.get(i, ()), *b.get(i, ())] for i in {*a, *b}}

        def walk(split, n0, per, it, tiles, after):
            for j in range(tiles):
                split(n0, per, it, j)
                for step in after.get(j + 1, ()):
                    step()

        def walk_ahead(split, n0, per, it, tiles, after):
            split(n0, per, it, 0)
            for j in range(tiles):
                if j + 1 < tiles:
                    split(n0, per, it, j + 1)
                for step in after.get(j + 1, ()):
                    step()

        def lru_steps(step, it):
            return {pos: [lambda k=k: step(it, k) for k in ks]
                    for pos, ks in ((3, (0,)), (4, (1,)), (5, (2, 3)), (6, (4,)), (7, (5,)))}

        def down_tile(d):
            return 16 + d // 2 * 4 + 2 + d % 2

        def dn_place(k, peeled):
            if peeled and k < 14:
                return ((5, 3), (6, 1), (6, 4), (6, 6), (7, 0), (7, 2), (7, 4), (7, 6), (7, 7),
                        (8, 1), (8, 2), (8, 4), (8, 6), (8, 7))[k]
            if k < 6:
                return ((1, 7), (2, 5), (3, 7), (4, 2), (4, 5), (4, 7))[k]
            return (5 + (k - 6) // 2, (3, 7)[k % 2]) if k < 18 else (11, 6)

        def dn_steps(step, h, peeled, late):
            steps = {}
            for k in range(19):
                pos = dn_place(k, peeled)[0] + 4
                if (pos > 12) == late:
                    steps.setdefault(pos - 12 * late, []).append(lambda k=k: step(h, k))
            return steps

        @block.scalar
        def _(act):
            ch = Chain(act, act_step)
            act.dma_start(PRM[:], A["params"]).then_inc(const_loaded, 16)
            act.dma_start(LH0[:], A["lru_h0"]).then_inc(const_loaded, 16)

            def split(n0, per, it, j):
                slot, use = (n0 + j) % RING, (n0 + j) // RING
                act.wait_ge(raw_full[slot], it * (16 * per // RING) + 16 * (use + 1))
                act.wait_ge(tile_used, it * per + (n0 + j + 1))
                act.activation(HI[:, slot * TILE:(slot + 1) * TILE], RAW[:, slot * TILE:(slot + 1) * TILE],
                               ACT.Copy).then_inc(hi_ready, 1)

            def root(n, rows=P):
                act.wait_ge(var_ready, n)
                act.activation(*n_root[n - 1], ACT.Sqrt).then_inc(sqrt_ready, 1)

            n_root = [(T1, T0), (ROW[5], ROW[4]), (ZRM[1], ZRM[0]), (T1, T0), (T1, T0)]

            act.wait_ge(const_loaded, 32)
            for k in range(KD):
                if k % 8 == 0:
                    split(0, 2, 0, k // 8)
                if k % 4 == 0:
                    act.wait_ge(x_loaded[k // 4], 16)
                if k >= 2:
                    act.wait_ge(sq_used, k - 1)
                act.activation(GS[:, k % 2 * N:(k % 2 + 1) * N], MG[:, k * N:(k + 1) * N], ACT.Square)
                act.activation(XH[:, k * N:(k + 1) * N], MG[:, k * N:(k + 1) * N], ACT.Copy,
                               scale=PRM[:, C_MIX + k:C_MIX + k + 1]).then_inc(xhi_ready, 1)

            def silu(strip):
                act.wait_ge(conv_ready, strip + 1)
                act.activation(TH, CV, ACT.Tanh).then_inc(th_ready, 1)

            def qkv(it, after):
                walk_ahead(split, QKV_N, 8, it, 8, joined(after, {8: [lambda: silu(it * 2)]}))

            def row_scalars(part):
                if part == 1:
                    act.wait_ge(row_c, 1)
                    act.activation(ROW[6], ROW[4], ACT.Ln)
                    act.activation(F16[:, 24:32], F16[:, 16:24], ACT.Ln).then_inc(row_d, 1)
                    return
                if part == 2:
                    act.wait_ge(row_e, 1)
                    act.activation(ROW[8], ROW[7], ACT.Exp, scale=-1.0).then_inc(row_f, 1)
                    return
                if part == 3:
                    act.wait_ge(row_cols, 1)
                    for c, n in enumerate((P, P, NS)):
                        ins = act.activation(COL[0:n, c * 56 + 48:c * 56 + 56], COL[0:n, c * 56 + 8:c * 56 + 16],
                                             ACT.Exp)
                    ins.then_inc(row_beg, 1)
                    return
                act.wait_ge(row_a, 1)
                act.activation(ROW[2], ROW[0], ACT.Tanh, scale=0.5)
                act.activation(ROW[3], ROW[1], ACT.Exp).then_inc(row_b, 1)
                act.activation(NSP[:], F16[:, 8:16], ACT.Exp)
                act.activation(SMALL[:, 3:4], PRM[:, C_ALOG:C_ALOG + 1], ACT.Exp).then_inc(row_b, 1)

            qkv(0, {2: [lambda: root(1)], 4: [lambda: row_scalars(0)], 5: [lambda: row_scalars(1)],
                    6: [lambda: row_scalars(2)]})
            with act.Fori(1, 6) as it:
                qkv(it, {4: [lambda: silu(it * 2 - 1)]})

            def qk_squares(i):
                if i == 0:
                    act.wait_ge(qkv_ready, 8)
                    act.wait_ge(xlo_ready, KD)
                for r in range(4 * i, 4 * i + 4):
                    if r >= 8:
                        act.wait_ge(sq_used, KD + r - 7)
                    act.activation(SQ8[:, r % 8 * N:(r % 8 + 1) * N], QKV[:, r * N:(r + 1) * N],
                                   ACT.Square).then_inc(qk_sq, 1)

            def lru_step(it, k):
                if k == 0:
                    act.wait_ge(gates_psum, it + 1)
                    for m in range(2):
                        act.activation(TR[:, m * N:(m + 1) * N], AX[2 * m][:, 0:N], ACT.Tanh, scale=0.5,
                                       bias=cols(PRM, it, 2, C_GA + m, 1))
                        ins = act.activation(TI[:, m * N:(m + 1) * N], AX[2 * m + 1][:, 0:N], ACT.Tanh, scale=0.5,
                                             bias=cols(PRM, it, 2, C_GX + m, 1))
                    ins.then_inc(gate_tanh, 1)
                elif k == 1:
                    act.wait_ge(la_ready, it + 1)
                    ch.link(act.activation(AA, TR, ACT.Exp))
                    act.activation(TH, TR, ACT.Tanh)
                    act.activation(G2, AA, ACT.Square).then_inc(a_ready, 1)
                elif k == 2:
                    act.wait_ge(m_ready, it + 1)
                    act.activation(TR, TH, ACT.Sqrt, scale=-1.0).then_inc(root_ready, 1)
                elif k == 3:
                    act.wait_ge(evacuated, it * 4 + (LRU_T + 4 + RING))
                    act.activation(G2, GL, ACT.Square).then_inc(gsq_ready, 1)
                elif k == 4:
                    act.wait_ge(gin_ready, it + 1)
                    act.activation(G2, G2, ACT.Tanh, scale=0.7978845608028654).then_inc(gth_ready, 1)
                else:
                    act.wait_ge(of_ready, it + 1)
                    act.activation(cols(OH, it, 2 * N), GL, ACT.Copy).then_inc(ohi_ready, 1)
                    act.wait_ge(lho_copied, it + 1)

            def lru(it, after):
                walk_ahead(split, LRU_N, 8, it, 8, after)

            lru(0, {**{i + 1: [lambda i=i: qk_squares(i)] for i in range(3)},
                    4: [lambda: silu(11), lambda: qk_squares(3)],
                    6: [lambda: row_scalars(3)], 7: [lambda: root(2)]})
            with act.Fori(1, 4) as it:
                ch.enter(it, 1, LINKS["rglru"])
                lru(it, lru_steps(lru_step, it - 1))
                ch.leave(3, "rglru")

            def gate(it, s, t0, g0):
                act.wait_ge(evacuated, it * 8 + (t0 + 4 * s + 2 + RING))
                act.activation(GS[:], GS[:], ACT.Tanh, scale=0.5).then_inc(gate_ready, 1)

            def dn_step(h, k):
                if k == 0:
                    act.wait_ge(bc_psum, h + 1)
                    act.wait_ge(dt_ready, h + 1)
                    act.activation(DTM, DTM, ACT.Exp).then_inc(dt_exp, 1)
                    act.activation(EG, AX[2][:, 0:N], ACT.Exp)
                    act.activation(VT, cols(QKV, h, N, V0), ACT.Copy).then_inc(vt_ready, 1)
                elif k == 1:
                    act.wait_ge(tok_psum, h + 1)
                    for c, n in enumerate((P, P, NS)):
                        act.activation(VB[0:n, c * P:(c + 1) * P], AX[2][0:n, c * P:(c + 1) * P], ACT.Copy,
                                       scale=cols(COL, h, 1, c * 56 + 16, 1, n))
                    act.wait_ge(lt_ready, h + 1)
                    for c, n in enumerate((P, P, NS)):
                        ins = act.activation(KDC[0:n, c * P:(c + 1) * P], AX[3][0:n, c * P:(c + 1) * P], ACT.Copy,
                                             scale=cols(COL, h, 1, c * 56 + 40, 1, n))
                    ins.then_inc(tok_scaled, 1)
                elif k == 15:
                    act.wait_ge(uw_psum, h + 1)
                    act.activation(W0, AX[0][:, 0:P], ACT.Copy)
                    act.activation(U12[:, 0:P], AX[0][:, P:2 * P], ACT.Copy)
                    act.activation(U12[0:NS, P:2 * P], AX[0][0:NS, 2 * P:3 * P], ACT.Copy)
                    act.activation(COMB[:, P:N], AX[1][:, P:N], ACT.Copy, scale=-1.0).then_inc(w0_ready, 1)
                elif k == 16:
                    act.wait_ge(s1_psum, h + 1)
                    act.activation(S1, AX[2][:, 0:P], ACT.Copy).then_inc(s1_ready, 1)

            def gated(it, n0, t0, h0, after, peeled=False):
                own = {8: [lambda: gate(it, 0, t0, 0)]}
                if h0 is not None:
                    own = joined(own, dn_steps(dn_step, it + h0, peeled, False))
                walk(split, n0, 12, it, 12, joined(after, own))

            def late(it, t0, h0):
                steps = {2: [lambda: gate(it, 1, t0, 0)]}
                return steps if h0 is None else joined(steps, dn_steps(dn_step, it + h0, False, True))

            gated(0, GPL_N, GPL_T, 0, lru_steps(lru_step, 3), True)
            with act.Fori(1, 4) as it:
                gated(it, GPL_N, GPL_T, 0, late(it - 1, GPL_T, 0))

            def pool_hi(g):
                act.wait_ge(of_ready, 4 + g + 1)
                act.activation(OH[:, 2 * g * N:2 * (g + 1) * N], DD, ACT.Copy).then_inc(ohi_ready, 1)

            walk(split, POOL_N, 16, 0, 16, {**late(3, GPL_T, 0), 12: [lambda: pool_hi(0)], 16: [lambda: pool_hi(1)]})
            gated(0, GPP_N, GPP_T, 4, {4: [lambda: pool_hi(2)], 8: [lambda: pool_hi(3)]}, True)
            with act.Fori(1, 4) as it:
                gated(it, GPP_N, GPP_T, 4, late(it - 1, GPP_T, 4))

            def o_squares():
                act.wait_ge(dn_done, HEADS)
                act.activation(OSQ, QKV[:, V0:V0 + 8 * N], ACT.Square).then_inc(osq_ready, 1)

            def z_gate(s):
                act.wait_ge(evacuated, Z_T + 2 * s + 2 + RING)
                act.activation(ZT, GS[:], ACT.Tanh, scale=0.5).then_inc(zr_tanh, 1)
                act.wait_ge(of_ready, 8 + s + 1)
                act.activation(OH[:, 2 * s * N:2 * (s + 1) * N], O1, ACT.Copy).then_inc(ohi_ready, 1)

            walk(split, Z_N, 16, 0, 16, {**late(3, GPP_T, 4), 4: [o_squares], 6: [lambda: root(3)],
                                         8: [lambda: z_gate(0)], 12: [lambda: z_gate(1)], 16: [lambda: z_gate(2)]})

            def merged_hi(strip):
                act.wait_ge(merged_ready, strip + 1)
                act.activation(cols(MH, strip, 2 * N), cols(MG, strip, 2 * N), ACT.Copy, scale=0.5) \
                    .then_inc(mhi_ready, 1)

            def gated_dn(it, after):
                walk(split, GPD_N, 12, it, 12, {**after, 8: [lambda: gate(it, 0, GPD_T, 0)],
                                                10: [lambda: merged_hi(it * 2)]})

            def late_dn(it):
                return {2: [lambda: gate(it, 1, GPD_T, 0)], 4: [lambda: merged_hi(it * 2 + 1)]}

            gated_dn(0, {4: [lambda: z_gate(3)]})
            with act.Fori(1, 4) as it:
                gated_dn(it, late_dn(it - 1))

            def residual(s):
                act.wait_ge(evacuated, s * 2 + (OUT_T + 2 + RING))
                if not isinstance(s, int) or s:
                    act.wait_ge(sq2_used, s)
                act.activation(GS[:], cols(X2, s, 2 * N), ACT.Square).then_inc(sq2_ready, 1)
                for m in range(2):
                    ins = act.activation(cols(XH, s, 2 * N, m * N, N), cols(X2, s, 2 * N, m * N, N), ACT.Copy,
                                         scale=cols(PRM, s, 2, C_MLP + m, 1))
                ins.then_inc(xh2_ready, 1)

            def out(it, after):
                walk(split, OUT_N, 8, it, 8, {**after, 8: [lambda: residual(it * 2)]})

            out(0, late_dn(3))
            with act.Fori(1, 4) as it:
                out(it, {4: [lambda: residual(it * 2 - 1)]})

            def relu2(it, s):
                act.wait_ge(evacuated, it * 24 + (MLP_T + 2 * s + 2 + RING))
                if not isinstance(it, int) or it * 4 + s:
                    act.wait_ge(hm_ready, it * 4 + s)
                ch.link(act.activation(HF, GS[:], ACT.Square))
                act.activation(OH[:, 2 * s * N:2 * (s + 1) * N], HF, ACT.Copy).then_inc(hf_ready, 1)

            def mlp(it, after):
                ups_ = {8 + 4 * s: [lambda s=s: relu2(it, s)] for s in range(4)}
                walk(split, MLP_N, 32, it, 32, {**ups_, **after})

            def last_squares(d):
                act.wait_ge(evacuated, 7 * 24 + MLP_T + 8 + 2 * d + 2 + RING)
                act.wait_ge(sq2_used, 8 + d)
                act.activation(GS[:], X2[:, 2 * d * N:2 * (d + 1) * N], ACT.Square).then_inc(sq2_ready, 1)

            mlp(0, {4: [lambda: residual(7)], 6: [lambda: root(4)]})
            with act.Fori(1, 7) as it:
                ch.enter(it, 1, LINKS["mlp"])
                mlp(it, {})
                ch.leave(6, "mlp")
            mlp(7, {down_tile(d) + 4: [lambda d=d: last_squares(d)] for d in range(6)})
            last_squares(6)
            last_squares(7)
            root(5)

        @block.vector
        def _(dve):
            ch = Chain(dve, dve_step)
            link = ch.link
            dve.sem_inc(lo_ready, RING)
            dve.sem_inc(evacuated, RING)

            def tt(out, a, b, op):
                return dve.tensor_tensor(out, a, b, op)

            def ts(out, a, s1, op0, s2=None, op1=None):
                return dve.tensor_scalar(out, a, s1, s2, op0, op1) if op1 is not None else \
                    dve.tensor_scalar(out, a, s1, None, op0)

            def stt(out, a, s, b, op0, op1):
                return dve.scalar_tensor_tensor(out=out, in0=a, scalar=s, in1=b, op0=op0, op1=op1)

            def split(n0, per, it, j):
                slot = (n0 + j) % RING
                dve.wait_ge(hi_ready, it * per + (n0 + j + 1))
                t = slice(slot * TILE, (slot + 1) * TILE)
                tt(LO[:, t], RAW[:, t], HI[:, t].bitcast(F32), ALU.subtract).then_inc(lo_ready, 1)

            def tile_done(n0, per, it, j):
                dve.wait_ge(tile_used, it * per + (n0 + j + 1 + RING))

            def rsqrt(n, ss, t0, t1, t2, out, inv_n, rows_scale=None):
                link(ts(t0, ss, inv_n, ALU.mult, EPS, ALU.add))
                dve.sem_inc(var_ready, 1)
                dve.wait_ge(sqrt_ready, n)
                link(dve.reciprocal(t1, t1))
                link(tt(t2, t1, t1, ALU.mult))
                link(tt(t2, t2, t0, ALU.mult))
                link(ts(t2, t2, -0.5, ALU.mult, 1.5, ALU.add))
                ins = tt(out, t1, t2, ALU.mult)
                if rows_scale is not None:
                    link(ins)
                    ins = ts(out, out, rows_scale, ALU.mult)
                return ins

            dve.wait_ge(const_loaded, 32)
            for lo, hi in ((C_CW, C_CW + 24 * CW), (C_GA, C_GX + KW), (C_DNW, C_DNW + 1)):
                ins = ts(PRM[:, lo:hi], PRM[:, lo:hi], 0.5, ALU.mult)
            link(ins)
            for k in range(KD):
                if k % 8 == 0:
                    split(0, 2, 0, k // 8)
                dve.wait_ge(xhi_ready, k + 1)
                c = slice(k * N, (k + 1) * N)
                stt(XL[:, c], MG[:, c], PRM[:, C_MIX + k:C_MIX + k + 1], XH[:, c].bitcast(F32),
                    ALU.mult, ALU.subtract).then_inc(xlo_ready, 1)

            def rms_first():
                dve.wait_ge(sq_used, KD)
                link(rsqrt(1, AX[0][:, 0:N], T0, T1, T2, R[:], 1.0 / D))

            def beta_a():
                tile_done(0, 2, 0, 1)
                link(tt(ROW[0], AX[3][0:16, 0:N], R[0:16, :], ALU.mult))

            def scaled(t, dst_prompt, dst_samples):
                b = MB[t % 4]
                tt(dst_prompt, b[:, 0:NP], R[:, 0:NP], ALU.mult)
                tt(dst_samples, b[:, NP:N].rearrange("p (b t) -> p b t", b=DB),
                   R[:, NP:N].rearrange("p (b t) -> p b t", b=DB), ALU.mult).then_inc(evacuated, 1)

            def conv(n0, per, it, j, t, tval, strip, first, ct, bias):
                tile_done(n0, per, it, j)
                if not first:
                    dve.wait_ge(tail_copied, strip)
                sv = [PAD[m][:, NP + 3:347].rearrange("p (b t) -> p b t", b=DB) for m in range(2)]
                for m in range(2):
                    scaled(t + m, PAD[m][:, 3:3 + NP], sv[m][:, :, CW - 1:CW - 1 + DT])
                dve.wait_ge(evacuated, tval)
                dve.wait_ge(prefix_ready, strip + 1)
                for w in range(CW):
                    for m in range(2):
                        k = cols(PRM, ct, CW, C_CW + m * CW + w, 1)
                        for src, dst in ((PAD[m][:, w:w + NP], CV[:, m * N:m * N + NP]),
                                         (sv[m][:, :, w:w + DT],
                                          CV[:, m * N + NP:(m + 1) * N].rearrange("p (b t) -> p b t", b=DB))):
                            if w:
                                ins = stt(dst, src, k, dst, ALU.mult, ALU.add)
                            elif bias is None:
                                ins = ts(dst, src, k, ALU.mult)
                            else:
                                ins = ts(dst, src, k, ALU.mult, bias[m], ALU.add)
                    if w < CW - 1:
                        link(ins)
                ins.then_inc(conv_ready, 1)

            def silu(it, s, first=False):
                strip = it * 2 + s
                conv(QKV_N, 8, it, 4 * s + 3, 2 * s, it * 4 + (QKV_T + 2 * s + 2 + RING), strip, first,
                     it * 4 + 2 * s, None)
                dve.wait_ge(th_ready, strip + 1)
                stt(cols(QKV, strip, 2 * N), TH, 1.0, CV, ALU.add, ALU.mult).then_inc(qkv_ready, 1)

            def qkv(it, after, first=False):
                walk(split, QKV_N, 8, it, 8, {**after, 8: [lambda: silu(it, 0, first)]})

            def rows_split(i, rows):
                c = slice(i * N, (i + 1) * N)
                link(dve.tensor_copy(RS[0:16, c], rows[0:16, :]))
                link(tt(RS[32:48, c], rows[0:16, :], RS[0:16, c].bitcast(F32), ALU.subtract))

            def row_scalars(part):
                z, nz, u, d, ln, sp_ = ROW[9], ROW[1], ROW[4], ROW[5], ROW[6], ROW[7]
                gam = z
                if part == 0:
                    link(ts(z, ROW[0], PRM[0:16, C_DTB:C_DTB + 1], ALU.add))
                    link(ts(nz, z, -1.0, ALU.mult))
                    tt(nz, z, nz, ALU.min)
                    link(ts(F16[:, 0:8], PRM[:, C_LAM:C_LAM + 8], -1.0, ALU.mult))
                    tt(F16[:, 8:16], F16[:, 0:8], PRM[:, C_LAM:C_LAM + 8], ALU.min).then_inc(row_a, 1)
                elif part == 1:
                    dve.wait_ge(row_b, 2)
                    ts(u, ROW[3], 1.0, ALU.add)
                    link(ts(F16[:, 16:24], NSP[:], 1.0, ALU.add))
                    dve.sem_inc(row_c, 1)
                    dve.reciprocal(ROW[8], u)
                    link(ts(d, u, -1.0, ALU.add))
                    link(tt(d, ROW[3], d, ALU.subtract))
                    link(tt(d, d, ROW[8], ALU.mult))
                    link(stt(d, z, 0.0, d, ALU.max, ALU.add))
                elif part == 2:
                    dve.wait_ge(row_d, 1)
                    link(tt(d, d, ln, ALU.add))
                    link(ts(d, d, SMALL[0:16, 3:4], ALU.mult, -1.0, ALU.mult))
                    link(dve.tensor_tensor_scan(gam, SEG, d, 0.0, ALU.mult, ALU.add))
                    for c in range(2):
                        ts(sp_[:, c * P:(c + 1) * P], gam[:, c * P:(c + 1) * P], gam[:, (c + 1) * P - 1:(c + 1) * P],
                           ALU.subtract)
                    g3 = gam[:, NP:N].rearrange("p (b t) -> p b t", b=DB)
                    link(tt(sp_[:, NP:N].rearrange("p (b t) -> p b t", b=DB), g3,
                            g3[:, :, DT - 1:DT].to_broadcast([16, DB, DT]), ALU.subtract))
                    dve.sem_inc(row_e, 1)
                    link(ts(ROW[2], ROW[2], 0.5, ALU.mult, 0.5, ALU.add))
                    link(ts(BG[0:16, :], gam, SMALL[0:16, 1:2], ALU.mult))
                    link(stt(BG[0:16, :], ROW[2], SMALL[0:16, 2:3], BG[0:16, :], ALU.mult, ALU.add))
                    rows_split(1, BG)
                    e, x = NSP[:], F16[:, 0:8]
                    link(ts(F16[:, 8:16], F16[:, 16:24], -1.0, ALU.add))
                    link(tt(F16[:, 8:16], e, F16[:, 8:16], ALU.subtract))
                    link(dve.reciprocal(F16[:, 16:24], F16[:, 16:24]))
                    link(tt(F16[:, 8:16], F16[:, 8:16], F16[:, 16:24], ALU.mult))
                    link(tt(F16[:, 8:16], F16[:, 8:16], F16[:, 24:32], ALU.add))
                    link(stt(F16[:, 8:16], x, 0.0, F16[:, 8:16], ALU.max, ALU.add))
                    link(ts(NSP[:], F16[:, 8:16], -4.0, ALU.mult))
                    dve.wait_ge(row_f, 1)
                    dve.sem_inc(row_g, 1)
                elif part == 3:
                    dve.wait_ge(row_psum, 1)
                    link(dve.tensor_copy(COL[:, 0:112].rearrange("p (c x) -> p c x", c=2)[:, :, 0:48],
                                         AX[0][:, 0:96].rearrange("p (c x) -> p c x", c=2)))
                    link(dve.tensor_copy(COL[0:NS, 112:160], AX[0][0:NS, 96:144]))
                    dve.sem_inc(row_cols, 1)
                    dve.wait_ge(row_beg, 1)
                    for c, n in enumerate((P, P, NS)):
                        b = c * 56
                        ins = tt(COL[0:n, b + 48:b + 56], COL[0:n, b + 48:b + 56], COL[0:n, b + 16:b + 24], ALU.mult)
                    link(ins)

            dve.wait_ge(masks_ready, 1)
            qkv(0, {2: [rms_first], 4: [beta_a, lambda: row_scalars(0)], 5: [lambda: row_scalars(1)],
                    6: [lambda: row_scalars(2)]}, True)
            with dve.Fori(1, 6) as it:
                ch.enter(it, 1, LINKS["qkv"])
                qkv(it, {4: [lambda: silu(it - 1, 1)]})
                ch.leave(5, "qkv")

            def row_norms():
                dve.wait_ge(sq_used, KD + 16)
                link(rsqrt(2, AX[1][0:16, 0:N], ROW[4], ROW[5], ROW[6], RN[0:16, :], 1.0, SMALL[0:16, 0:1]))
                rows_split(0, RN)
                dve.sem_inc(row_beg, 1)

            def lru_conv(it):
                conv(LRU_N, 8, it, 3, 0, it * 4 + (LRU_T + 2 + RING), it + 12, False, it * 2 + 24,
                     [cols(PRM, it, 2, C_CB + m, 1) for m in range(2)])

            def lru_step(it, k):
                if k == 0:
                    dve.wait_ge(gate_tanh, it + 1)
                    for m in range(2):
                        c = slice(m * N, (m + 1) * N)
                        ins = ts(TR[:, c], TR[:, c], 1.0, ALU.add, cols(NSP, it, 2, m, 1), ALU.mult)
                    ins.then_inc(la_ready, 1)
                    stt(TI, TI, 1.0, CV, ALU.add, ALU.mult)
                elif k == 1:
                    dve.wait_ge(a_ready, it + 1)
                    stt(TH, G2, 1.0, TH, ALU.add, ALU.mult).then_inc(m_ready, 1)
                elif k == 2:
                    dve.wait_ge(root_ready, it + 1)
                    link(stt(TI, TR, 0.5, TI, ALU.mult, ALU.mult))
                    for m in range(2):
                        first = slice(m * N + NP, (m + 1) * N, DT)
                        ins = tt(G2[:, m * DB:(m + 1) * DB], AA[:, first],
                                 cols(LH0, it, 2 * DB, m * DB, DB), ALU.mult)
                    link(ins)
                    for m in range(2):
                        first = slice(m * N + NP, (m + 1) * N, DT)
                        tt(TI[:, first], TI[:, first], G2[:, m * DB:(m + 1) * DB], ALU.add)
                        ins = dve.memset(AA[:, first], 0.0)
                    link(ins)
                    for m in range(2):
                        c = slice(m * N, (m + 1) * N)
                        ins = dve.tensor_tensor_scan(TR[:, c], AA[:, c], TI[:, c], 0.0, ALU.mult, ALU.add)
                    ins.then_inc(h_ready, 1)
                elif k == 3:
                    tile_done(LRU_N, 8, it, 7)
                    for m in range(2):
                        tt(GL[:, m * N:(m + 1) * N], MB[2 + m][:, 0:N], R[:], ALU.mult).then_inc(evacuated, 1)
                elif k == 4:
                    dve.wait_ge(gsq_ready, it + 1)
                    link(ts(G2, G2, 0.044715, ALU.mult, 1.0, ALU.add))
                    tt(G2, G2, GL, ALU.mult).then_inc(gin_ready, 1)
                else:
                    dve.wait_ge(gth_ready, it + 1)
                    link(stt(GL, G2, 1.0, GL, ALU.add, ALU.mult))
                    dve.wait_ge(h_ready, it + 1)
                    stt(GL, TR, 0.5, GL, ALU.mult, ALU.mult).then_inc(of_ready, 1)
                    dve.wait_ge(ohi_ready, it + 1)
                    tt(cols(OL, it, 2 * N), GL, cols(OH, it, 2 * N).bitcast(F32), ALU.subtract).then_inc(o_ready, 1)

            def lru(it, after):
                walk(split, LRU_N, 8, it, 8, {**after, 8: [lambda: lru_conv(it)]})

            lru(0, {4: [lambda: silu(5, 1)], 6: [lambda: row_scalars(3)], 7: [row_norms]})
            with dve.Fori(1, 4) as it:
                ch.enter(it, 1, LINKS["lru"])
                lru(it, lru_steps(lru_step, it - 1))
                ch.leave(3, "lru")

            def gate(n0, t0, it, s):
                tile_done(n0, 12, it, 6 * s + 3)
                dve.wait_ge(evacuated, it * 8 + (t0 + 4 * s + RING))
                for m in range(2):
                    tt(GS[:, m * N:(m + 1) * N], MB[m][:, 0:N], R[:], ALU.mult).then_inc(evacuated, 1)

            def merge(n0, t0, g0, it, s, branch):
                tile_done(n0, 12, it, 6 * s + 5)
                dve.wait_ge(gate_ready, it * 2 + (g0 + s + 1))
                for m in range(2):
                    dst = GS[:, m * N:(m + 1) * N] if branch else cols(MG, it, 4 * N, (2 * s + m) * N, N)
                    stt(dst, GS[:, m * N:(m + 1) * N], 1.0, MB[2 + m][:, 0:N], ALU.add, ALU.mult) \
                        .then_inc(evacuated, 1)
                if not branch:
                    return
                dve.wait_ge(evacuated, it * 8 + (t0 + 4 * s + 4 + RING))
                sums = cols(MG, it, 4 * N, 2 * s * N, 2 * N)
                ins = tt(sums, sums, GS[:], ALU.add)
                if branch == 1:
                    link(ins)
                    return
                ins.then_inc(merged_ready, 1)
                dve.wait_ge(mhi_ready, it * 2 + (s + 1))
                stt(cols(ML, it, 4 * N, 2 * s * N, 2 * N), sums, 0.5,
                    cols(MH, it, 4 * N, 2 * s * N, 2 * N).bitcast(F32), ALU.mult, ALU.subtract) \
                    .then_inc(mlo_ready, 1)

            both = ((P, slice(0, NP), True), (NS, slice(NP, N), False))

            def dn_step(h, k):
                if k == 0:
                    dve.wait_ge(bc_psum, h + 1)
                    for c, (n, lo, hi) in enumerate(((P, 0, P), (P, P, 2 * P), (NS, NP, N))):
                        ins = ts(DTM[0:n, lo:hi], AX[2][0:n, lo:hi], cols(COL, h, 1, c * 56 + 8, 1, n),
                                 ALU.subtract, 0.0, ALU.min)
                    ins.then_inc(dt_ready, 1)
                    link(tt(KT, cols(QKV, h, N, 8 * N), AX[0][:, 0:N], ALU.mult))
                    tt(QT, cols(QKV, h, N), AX[1][:, 0:N], ALU.mult)
                    tt(KB, KT, AX[3][:, 0:N], ALU.mult).then_inc(khat_ready, 1)
                elif k == 1:
                    dve.wait_ge(tok_psum, h + 1)
                    for c, n in enumerate((P, P, NS)):
                        ts(KBG[0:n, c * P:(c + 1) * P], AX[3][0:n, c * P:(c + 1) * P],
                           cols(COL, h, 1, c * 56 + 48, 1, n), ALU.mult)
                    dve.wait_ge(dtm_ready, h + 1)
                    for n, c, _ in both:
                        tt(LT[0:n, c], AX[0][0:n, c], DTM[0:n, c], ALU.mult)
                        ins = tt(QKD[0:n, c], AX[1][0:n, c], DTM[0:n, c], ALU.mult)
                    link(ins)
                    m = M1T[:, None, :].to_broadcast([P, 2, P])
                    tt(YY[:, 0:NP].rearrange("p (c i) -> p c i", c=2), LT[:, 0:NP].rearrange("p (c i) -> p c i", c=2),
                       m, ALU.mult)
                    link(tt(YY[0:NS, NP:N], LT[0:NS, NP:N], M1T[0:NS, 0:NS], ALU.mult))
                    idb = ident[:, None, :].to_broadcast([P, 2, P])
                    tt(XT[:, 0:NP].rearrange("p (c i) -> p c i", c=2), idb,
                       YY[:, 0:NP].rearrange("p (c i) -> p c i", c=2), ALU.subtract)
                    tt(XT[0:NS, NP:N], ident[0:NS, 0:NS], YY[0:NS, NP:N], ALU.subtract).then_inc(lt_ready, 1)
                elif k == 2:
                    dve.wait_ge(xt_psum, h + 1)
                    dve.tensor_copy(XX[:, 0:NP], AX[0][:, 0:NP])
                    dve.tensor_copy(XX[0:NS, NP:N], AX[0][0:NS, NP:N]).then_inc(x_ready, 1)
                elif k < 15 and k % 2:
                    level = (k - 3) // 2
                    dve.wait_ge(y_psum, h * 6 + (level + 1))
                    m = LM[:, level * P:(level + 1) * P]
                    ins = tt(YY[:, 0:NP].rearrange("p (c i) -> p c i", c=2),
                             AX[1][:, 0:NP].rearrange("p (c i) -> p c i", c=2),
                             m[:, None, :].to_broadcast([P, 2, P]), ALU.mult)
                    if level < 2:
                        ins = tt(YY[0:NS, NP:N], AX[1][0:NS, NP:N], m[0:NS, 0:NS], ALU.mult)
                    ins.then_inc(y_ready, 1)
                elif k < 15:
                    level = (k - 4) // 2
                    dve.wait_ge(z_psum, h * 6 + (level + 1))
                    for n, c, prompt in both:
                        if prompt or level < 2:
                            if level < 5:
                                tt(XX[0:n, c], XX[0:n, c], AX[2][0:n, c], ALU.subtract)
                            ins = tt(XT[0:n, c], XT[0:n, c], AX[3][0:n, c], ALU.subtract)
                    ins.then_inc(x_ready, 1)
                elif k == 16:
                    dve.wait_ge(s1_psum, h + 1)
                    dve.wait_ge(s1_ready, h + 1)
                    dve.tensor_copy(WS, AX[2][:, 2 * P:3 * P]).then_inc(ws_ready, 1)
                elif k == 17:
                    dve.wait_ge(w1_psum, h + 1)
                    tt(U12[:, 0:P], U12[:, 0:P], AX[1][:, P:2 * P], ALU.add)
                    link(tt(U12[0:NS, P:2 * P], U12[0:NS, P:2 * P], AX[1][0:NS, 2 * P:3 * P], ALU.add))
                    tt(WX.rearrange("p (b v) -> p b v", b=DB), U12[0:NS, None, P:2 * P].to_broadcast([NS, DB, P]),
                       BM[0:NS, :, None].to_broadcast([NS, DB, P]), ALU.mult).then_inc(w_ready, 1)
                elif k == 18:
                    dve.wait_ge(fin_psum, h + 1)
                    dve.tensor_copy(cols(QKV, h, N, V0, NP), AX[3][:, 0:NP])
                    tt(cols(QKV, h, N, V0 + NP, NS), AX[3][:, NP:N], WS[:, NS:2 * NS], ALU.add)
                    stt(S1, S1, EG[:, NP - 1:NP], AX[2][:, 0:P], ALU.mult, ALU.add)
                    for b in range(DB):
                        t = NP + DT * b + DT - 1
                        c = slice(b * P, (b + 1) * P)
                        ins = stt(SS[:, c], SS[:, c], EG[:, t:t + 1], AX[b // 4][:, b % 4 * P:(b % 4 + 1) * P],
                                  ALU.mult, ALU.add)
                    ins.then_inc(dn_done, 1)

            def gated(it, n0, t0, g0, h0, branch, after, peeled=False):
                own = {8: [lambda: gate(n0, t0, it, 0)], 10: [lambda: merge(n0, t0, g0, it, 0, branch)]}
                if h0 is not None:
                    own = joined(own, dn_steps(dn_step, it + h0, peeled, False))
                walk(split, n0, 12, it, 12, joined(after, own))

            def late(it, n0, t0, g0, h0, branch):
                steps = {2: [lambda: gate(n0, t0, it, 1)], 4: [lambda: merge(n0, t0, g0, it, 1, branch)]}
                return steps if h0 is None else joined(steps, dn_steps(dn_step, it + h0, False, True))

            gated(0, GPL_N, GPL_T, 0, 0, 0, lru_steps(lru_step, 3), True)
            with dve.Fori(1, 4) as it:
                ch.enter(it, 1, LINKS["gpl"])
                gated(it, GPL_N, GPL_T, 0, 0, 0, late(it - 1, GPL_N, GPL_T, 0, 0, 0))
                ch.leave(3, "gpl")

            ups = UP.rearrange("p (m c) -> p m c", m=2)

            def pool_sums(g):
                w = 2 << g
                tile_done(POOL_N, 16, 0, 4 * g + 3)
                if g == 0:
                    dve.wait_ge(ss_stored, 4 * 32)
                if g:
                    dve.wait_ge(ptail_copied, g)
                for m in range(2):
                    scaled(2 * g + m, ups[:, m, PB:PB + NP],
                           ups[:, m, PB + NP:455].rearrange("p (b t) -> p b t", b=DB)[:, :, PB:PB + DT])
                dve.wait_ge(evacuated, POOL_T + 2 * g + 2 + RING)
                dve.wait_ge(pfx_ready, g + 1)
                src = ups
                for i in range(g + 1):
                    dst = (SA, SB_)[i % 2].rearrange("p (m c) -> p m c", m=2)
                    lo, s = (2 << i) - 1, 1 << i
                    link(tt(dst[:, :, lo:455], src[:, :, lo:455], src[:, :, lo - s:455 - s], ALU.add))
                    src = dst
                link(tt(F16[:].rearrange("p (m c) -> p m c", m=2), src[:, :, PB:PB + 16],
                        RC[:, None, 16 * g:16 * (g + 1)].to_broadcast([P, 2, 16]), ALU.mult))
                for m in range(2):
                    tt(DD[:, m * N:m * N + 16], F16[:, 16 * m:16 * (m + 1)], ups[:, m, PB:PB + 16], ALU.subtract)
                    stt(DD[:, m * N + 16:m * N + NP], src[:, m, PB + 16:PB + NP], 1.0 / w,
                        ups[:, m, PB + 16:PB + NP], ALU.mult, ALU.subtract)
                    v3 = lambda t: t[:, m, PB + NP:455].rearrange("p (b t) -> p b t", b=DB)[:, :, PB:PB + DT]
                    ins = stt(DD[:, m * N + NP:(m + 1) * N].rearrange("p (b t) -> p b t", b=DB), v3(src), 1.0 / w,
                              v3(ups), ALU.mult, ALU.subtract)
                ins.then_inc(d_ready, 1)

            def pool_out(g):
                dve.wait_ge(py_psum, g + 1)
                for m in range(2):
                    c = 2 * g + m
                    ins = ts(DD[:, m * N:(m + 1) * N], AX[m][:, 0:N], PRM[:, C_PS + c:C_PS + c + 1], ALU.mult)
                ins.then_inc(of_ready, 1)
                dve.wait_ge(ohi_ready, 4 + g + 1)
                c = slice(2 * g * N, 2 * (g + 1) * N)
                tt(OL[:, c], DD, OH[:, c].bitcast(F32), ALU.subtract).then_inc(o_ready, 1)

            steps = late(3, GPL_N, GPL_T, 0, 0, 0)
            steps[8] = [lambda: pool_sums(0)]
            for g in (1, 2):
                steps[8 + 4 * g] = [lambda g=g: pool_out(g - 1), lambda g=g: pool_sums(g)]
            walk(split, POOL_N, 16, 0, 16, steps)
            gated(0, GPP_N, GPP_T, 8, 4, 1, {4: [lambda: pool_out(2), lambda: pool_sums(3)], 8: [lambda: pool_out(3)]},
                  True)
            with dve.Fori(1, 4) as it:
                ch.enter(it, 1, LINKS["gpp"])
                gated(it, GPP_N, GPP_T, 8, 4, 1, late(it - 1, GPP_N, GPP_T, 8, 4, 1))
                ch.leave(3, "gpp")

            def o_norm():
                dve.wait_ge(o_ss_psum, 1)
                rsqrt(3, AX[2][0:16, 0:N], ZRM[0], ZRM[1], RT[0][0:16], RO, 1.0 / P).then_inc(ro_ready, 1)

            def z_out(s):
                tile_done(Z_N, 16, 0, 4 * s + 3)
                for m in range(2):
                    tt(GS[:, m * N:(m + 1) * N], MB[2 * (s % 2) + m][:, 0:N], R[:], ALU.mult).then_inc(evacuated, 1)
                dve.wait_ge(zb_psum, s + 1)
                for m in range(2):
                    c = V0 + (2 * s + m) * N
                    ins = tt(O1[:, m * N:(m + 1) * N], QKV[:, c:c + N], AX[m][:, 0:N], ALU.mult)
                link(ins)
                dve.wait_ge(zr_tanh, s + 1)
                link(stt(ZT, ZT, 1.0, GS[:], ALU.add, ALU.mult))
                stt(O1, O1, PRM[:, C_DNW:C_DNW + 1], ZT, ALU.mult, ALU.mult).then_inc(of_ready, 1)
                dve.wait_ge(ohi_ready, 8 + s + 1)
                c = slice(2 * s * N, 2 * (s + 1) * N)
                tt(OL[:, c], O1, OH[:, c].bitcast(F32), ALU.subtract).then_inc(o_ready, 1)

            steps = late(3, GPP_N, GPP_T, 8, 4, 1)
            steps[6] = [o_norm]
            for s in range(3):
                steps[8 + 4 * s] = [lambda s=s: z_out(s)]
            walk(split, Z_N, 16, 0, 16, steps)
            dve.wait_ge(ss_stored, HEADS * 32)
            gated(0, GPD_N, GPD_T, 16, None, 2, {4: [lambda: z_out(3)]})
            with dve.Fori(1, 4) as it:
                gated(it, GPD_N, GPD_T, 16, None, 2, late(it - 1, GPD_N, GPD_T, 16, None, 2))

            def residual(it, s):
                tile_done(OUT_N, 8, it, 4 * s + 3)
                if isinstance(it, int) and it == 0 and s == 0:
                    dve.wait_ge(x2_loaded, 16)
                for m in range(2):
                    x = cols(X2, it, 4 * N, (2 * s + m) * N, N)
                    tt(x, MB[2 * s + m][:, 0:N], x, ALU.add).then_inc(evacuated, 1)
                dve.wait_ge(xh2_ready, it * 2 + (s + 1))
                for m in range(2):
                    ins = stt(cols(XL, it, 4 * N, (2 * s + m) * N, N), cols(X2, it, 4 * N, (2 * s + m) * N, N),
                              cols(PRM, it, 4, C_MLP + 2 * s + m, 1),
                              cols(XH, it, 4 * N, (2 * s + m) * N, N).bitcast(F32), ALU.mult, ALU.subtract)
                ins.then_inc(xg2_ready, 1)

            def out(it, after):
                walk(split, OUT_N, 8, it, 8, {**after, 8: [lambda: residual(it, 0)]})

            out(0, late(3, GPD_N, GPD_T, 16, None, 2))
            with dve.Fori(1, 4) as it:
                out(it, {4: [lambda: residual(it - 1, 1)]})

            def rms_mlp():
                dve.wait_ge(sq2_used, 8)
                link(rsqrt(4, AX[0][:, 0:N], T0, T1, T2, R[:], 1.0 / D))

            def relu2(it, s):
                tile_done(MLP_N, 32, it, 4 * s + 3)
                for m in range(2):
                    stt(GS[:, m * N:(m + 1) * N], MB[2 * (s % 2) + m][:, 0:N], 0.0, R[:], ALU.max, ALU.mult) \
                        .then_inc(evacuated, 1)
                dve.wait_ge(hf_ready, it * 4 + (s + 1))
                c = slice(2 * s * N, 2 * (s + 1) * N)
                tt(OL[:, c], HF, OH[:, c].bitcast(F32), ALU.subtract).then_inc(hm_ready, 1)

            def down(it, d):
                tile_done(MLP_N, 32, it, down_tile(d))
                for m in range(2):
                    x = X2[:, (2 * d + m) * N:(2 * d + m + 1) * N]
                    tt(x, MB[2 * (d % 2) + m][:, 0:N], x, ALU.add).then_inc(evacuated, 1)

            def mlp(it, after):
                own = {8 + 4 * s: [lambda s=s: relu2(it, s)] for s in range(4)}
                own.update({down_tile(d) + 4: [lambda d=d: down(it, d)] for d in range(6)})
                walk(split, MLP_N, 32, it, 32, {**own, **after})

            mlp(0, {4: [lambda: residual(3, 1)], 6: [rms_mlp]})
            with dve.Fori(1, 7) as it:
                mlp(it, {2: [lambda: down(it - 1, 6)], 3: [lambda: down(it - 1, 7)]})
            mlp(7, {2: [lambda: down(6, 6)], 3: [lambda: down(6, 7)]})
            down(7, 6)
            down(7, 7)

            dve.wait_ge(sq2_used, 16)
            link(rsqrt(5, AX[0][:, 0:N], T0, T1, T2, R[:], 1.0 / D))
            for k in range(KD):
                c = slice(k * N, (k + 1) * N)
                stt(MG[:, c], X2[:, c], PRM[:, C_FIN + k:C_FIN + k + 1], R[:], ALU.mult, ALU.mult) \
                    .then_inc(out_ready, 1)

        @block.tensor
        def _(pe):
            pe.sem_inc(tile_used, RING)

            def product(bank, hi, lo, xh, xl, first, last):
                pe.matmul(bank, hi, xh, start=first, stop=False)
                pe.matmul(bank, hi, xl, start=False, stop=False)
                return pe.matmul(bank, lo, xh, start=False, stop=last)

            def tile(n0, per, t0, tper, it, j, t, kb, blocks, xh, xl, wait=None, between=()):
                slot = (n0 + j) % RING
                pe.wait_ge(lo_ready, it * per + (n0 + j + 1 + RING))
                if wait is not None:
                    pe.wait_ge(*wait)
                for m in range(2):
                    if kb == 0:
                        pe.wait_ge(evacuated, it * tper + (t0 + t + m + 1))
                    for k in range(4):
                        at = slot * TILE + k * 256 + m * P
                        x = slice((kb + k) * N, (kb + k + 1) * N)
                        ins = product(MB[(t + m) % 4][:, 0:N], HI[:, at:at + P], LO[:, at:at + P],
                                      xh[:, x], xl[:, x], kb + k == 0, kb + k == blocks - 1)
                        for b, step in between:
                            if b == 4 * m + k and b < 7:
                                step()
                ins.then_inc(tile_used, 1)
                for b, step in between:
                    if b == 7:
                        step()

            pe.wait_ge(ones_ready, 1)
            for j in range(2):
                pe.wait_ge(lo_ready, j + 1 + RING)
                for k in range(8 * j, 8 * j + 8):
                    pe.wait_ge(xlo_ready, k + 1)
                    x = slice(k * N, (k + 1) * N)
                    at = j * TILE + k % 8 * P
                    ins = product(AX[3][:, 0:N], HI[:, at:at + P], LO[:, at:at + P], XH[:, x], XL[:, x],
                                  k == 0, k == KD - 1)
                    if k % 8 == 7:
                        ins.then_inc(tile_used, 1)
                    pe.matmul(AX[0][:, 0:N], ones[:], GS[:, k % 2 * N:(k % 2 + 1) * N],
                              start=k == 0, stop=k == KD - 1).then_inc(sq_used, 1)

            def strip(n0, per, t0, tper, it, j, t, xh, xl, waits=None, tiles=4, between=None):
                for i in range(tiles):
                    tile(n0, per, t0, tper, it, j + i, t, 4 * i, 4 * tiles, xh, xl,
                         None if waits is None else waits(i), (between or {}).get(j + i, ()))

            def turn_rows():
                pe.wait_ge(row_g, 1)
                for c, (n, lo, hi) in enumerate(((P, 0, P), (P, P, 2 * P), (NS, NP, N))):
                    for i, row in enumerate((ROW[9], ROW[2], ROW[8])):
                        ins = pe.transpose(AX[0][0:n, c * 48 + i * 16:c * 48 + (i + 1) * 16], row[:, lo:hi],
                                           ident[0:16, 0:16])
                ins.then_inc(row_psum, 1)

            def qkv(it):
                for s in range(2):
                    strip(QKV_N, 8, QKV_T, 4, it, 4 * s, 2 * s, XH, XL)

            qkv(0)
            with pe.Fori(1, 6) as it:
                qkv(it)

            def qk_sums(i):
                if i == 0:
                    pe.wait_ge(qkv_ready, 8)
                    pe.wait_ge(masks_ready, 1)
                for r in range(4 * i, 4 * i + 4):
                    pe.wait_ge(qk_sq, r + 1)
                    pe.matmul(AX[1][0:16, 0:N], EONE[:, 15 - r:31 - r], SQ8[:, r % 8 * N:(r % 8 + 1) * N],
                              start=r == 0, stop=r == 15).then_inc(sq_used, 1)

            def gates(it):
                pe.wait_ge(gw_loaded, it * 16 + 16)
                pe.wait_ge(conv_ready, it + 13)
                if isinstance(it, int) and it == 0:
                    pe.wait_ge(row_beg, 2)
                for m in range(2):
                    for g in range(2):
                        ins = pe.matmul(AX[2 * m + g][:, 0:N], GWT[:, (2 * m + g) * P:(2 * m + g + 1) * P],
                                        CV[:, m * N:(m + 1) * N], start=True, stop=True)
                ins.then_inc(gates_psum, 1)

            def lru(it, between):
                strip(LRU_N, 8, LRU_T, 4, it, 0, 0, XH, XL, between=between)
                strip(LRU_N, 8, LRU_T, 4, it, 4, 2, XH, XL, between=between)

            lru(0, {0: [(7, lambda: qk_sums(0))], 1: [(7, lambda: qk_sums(1)), (7, turn_rows)], 2: [(7, lambda: qk_sums(2))],
                    3: [(7, lambda: qk_sums(3))], 7: [(7, lambda: gates(0))]})
            with pe.Fori(1, 4) as it:
                lru(it, {7: [(7, lambda: gates(it))]})

            units = ((P, 0, P), (P, P, 2 * P), (NS, NP, N))

            def dn_step(h, k, first):
                def mm(out, a, b):
                    return pe.matmul(out, a, b, start=True, stop=True)

                if k == 0:
                    pe.wait_ge(rm_ready, h + 1)
                    if first:
                        pe.wait_ge(o_ready, first)
                    if not (isinstance(h, int) and h == 0):
                        pe.wait_ge(dn_done, h)
                    lo, hi = SELS[0:48, 0:P], SELS[0:48, P:2 * P]
                    mm(AX[2][:, 0:N], hi, RM[1])
                    mm(AX[0][:, 0:N], hi, RM[0])
                    mm(AX[1][:, 0:N], lo, RM[0])
                    mm(AX[3][:, 0:N], lo, RM[1]).then_inc(bc_psum, 1)
                elif k == 1:
                    pe.wait_ge(khat_ready, h + 1)
                    pe.wait_ge(vt_ready, h + 1)
                    for n, lo, hi in units:
                        mm(AX[0][0:n, lo:hi], KT[:, lo:hi], KB[:, lo:hi])
                        mm(AX[1][0:n, lo:hi], KT[:, lo:hi], QT[:, lo:hi])
                    for c, (n, lo, hi) in enumerate(units):
                        pe.transpose(AX[2][0:n, c * P:(c + 1) * P], VT[:, lo:hi], ident[:])
                        ins = pe.transpose(AX[3][0:n, c * P:(c + 1) * P], KT[:, lo:hi], ident[:])
                    ins.then_inc(tok_psum, 1)
                elif k == 2:
                    pe.wait_ge(lt_ready, h + 1)
                    for n, lo, hi in units:
                        ins = pe.transpose(AX[0][0:n, lo:hi], XT[0:n, lo:hi], ident[0:n, 0:n])
                    ins.then_inc(xt_psum, 1)
                elif k < 15 and k % 2:
                    level = (k - 3) // 2
                    pe.wait_ge(x_ready, h * 7 + (level + 1))
                    for n, lo, hi in units[:3 if level < 2 else 2]:
                        ins = mm(AX[1][0:n, lo:hi], LT[0:n, lo:hi], XX[0:n, lo:hi])
                    ins.then_inc(y_psum, 1)
                elif k < 15:
                    level = (k - 4) // 2
                    pe.wait_ge(y_ready, h * 6 + (level + 1))
                    if level == 0:
                        pe.wait_ge(tok_scaled, h + 1)
                    for n, lo, hi in units[:3 if level < 2 else 2]:
                        if level < 5:
                            mm(AX[2][0:n, lo:hi], XT[0:n, lo:hi], YY[0:n, lo:hi])
                        ins = mm(AX[3][0:n, lo:hi], YY[0:n, lo:hi], XT[0:n, lo:hi])
                    ins.then_inc(z_psum, 1)
                elif k == 15:
                    pe.wait_ge(x_ready, h * 7 + 7)
                    for c, (n, lo, hi) in enumerate(units):
                        mm(AX[0][0:n, c * P:(c + 1) * P], XT[0:n, lo:hi], VB[0:n, c * P:(c + 1) * P])
                    for c in (1, 2):
                        n, lo, hi = units[c]
                        ins = mm(AX[1][:, lo:hi], KBG[0:n, c * P:(c + 1) * P], XT[0:n, lo:hi])
                    ins.then_inc(uw_psum, 1)
                elif k == 16:
                    pe.wait_ge(w0_ready, h + 1)
                    pe.wait_ge(qg_ready, h + 1)
                    pe.wait_ge(ss_loaded, h * 16 + 16)
                    mm(AX[3][:, 0:P], W0, QKD[:, 0:P])
                    for b in range(DB):
                        c = slice(NP + DT * b, NP + DT * (b + 1))
                        mm(AX[2][:, 2 * P:3 * P].rearrange("p (a t) -> p a t", a=2)[:, :, DT * b:DT * (b + 1)],
                           SS[:, b * P:(b + 1) * P], COMB.rearrange("p (a t) -> p a t", a=2)[:, :, c])
                    mm(AX[2][:, 0:P], KDC[:, 0:P], W0).then_inc(s1_psum, 1)
                elif k == 17:
                    pe.wait_ge(s1_ready, h + 1)
                    pe.wait_ge(ws_ready, h + 1)
                    mm(AX[1][:, P:2 * P], COMB[:, P:2 * P], S1)
                    pe.transpose(AX[1][0:NS, 2 * P:3 * P], WS[:, 0:NS], ident[:]).then_inc(w1_psum, 1)
                elif k == 18:
                    pe.wait_ge(w_ready, h + 1)
                    pe.matmul(AX[3][:, P:2 * P], S1, COMB[:, N + P:N + 2 * P], start=True, stop=False)
                    pe.matmul(AX[3][:, P:2 * P], U12[:, 0:P], QKD[:, P:2 * P], start=False, stop=True)
                    mm(AX[3][:, NP:N], U12[0:NS, P:2 * P], QKD[0:NS, NP:N])
                    mm(AX[2][:, 0:P], KDC[:, P:2 * P], U12[:, 0:P])
                    for i in range(2):
                        ins = mm(AX[i][:, 0:512], KDC[0:NS, 2 * P:3 * P], WX[:, 512 * i:512 * (i + 1)])
                    ins.then_inc(fin_psum, 1)

            def gated(it, n0, t0, h0, first, o0, between=None):
                between = dict(between or {})
                if h0 is not None:
                    for k in range(19):
                        j, b = dn_place(k, first is not None)
                        between[j] = list(between.get(j, ())) + [(b, lambda k=k: dn_step(it + h0, k, first))]
                for s in range(2):
                    strip(n0, 12, t0, 8, it, 6 * s, 4 * s, XH, XL, between=between)
                    strip(n0, 12, t0, 8, it, 6 * s + 4, 4 * s + 2, OH, OL,
                          waits=(lambda i: (o_ready, o0 + 2 * (i + 1))) if first is not None and s == 0 else None,
                          tiles=2, between=between)

            gated(0, GPL_N, GPL_T, 0, 4, 0)
            with pe.Fori(1, 4) as it:
                gated(it, GPL_N, GPL_T, 0, None, 0)

            def pool_product(g):
                pe.wait_ge(d_ready, g + 1)
                if g == 0:
                    pe.wait_ge(pool_loaded, 32)
                    pe.wait_ge(dn_done, 4)
                else:
                    pe.wait_ge(o_ready, 4 + g)
                for m in range(2):
                    for k in range(2):
                        at = (2 * g + k) * GW_ + m * P
                        ins = pe.matmul(AX[m][:, 0:N], PW[:, at:at + P], DD[:, k * N:(k + 1) * N],
                                        start=k == 0, stop=k == 1)
                ins.then_inc(py_psum, 1)

            for g in range(GROUPS):
                strip(POOL_N, 16, POOL_T, 8, 0, 4 * g, 2 * g, XH, XL,
                      between={7: [(7, lambda: pool_product(0))], 11: [(7, lambda: pool_product(1))],
                               15: [(7, lambda: pool_product(2))]})
            gated(0, GPP_N, GPP_T, 4, 8, 4, {3: [(7, lambda: pool_product(3))]})
            with pe.Fori(1, 4) as it:
                gated(it, GPP_N, GPP_T, 4, None, 4)

            def o_sums():
                pe.wait_ge(osq_ready, 1)
                pe.wait_ge(dn_done, HEADS)
                for h in range(HEADS):
                    ins = pe.matmul(AX[2][0:16, 0:N], EONE[:, 15 - h:31 - h], OSQ[:, h * N:(h + 1) * N],
                                    start=h == 0, stop=h == HEADS - 1)
                ins.then_inc(o_ss_psum, 1)

            def z_rows(s):
                pe.wait_ge(zm_ready, s + 1)
                if s:
                    pe.wait_ge(o_ready, 8 + s)
                for m in range(2):
                    ins = pe.matmul(AX[m][:, 0:N], ones[0:16, :], ZRM[m], start=True, stop=True)
                ins.then_inc(zb_psum, 1)

            for s in range(4):
                strip(Z_N, 16, Z_T, 8, 0, 4 * s, 2 * s, XH, XL,
                      between={1: [(7, o_sums)], 5: [(7, lambda: z_rows(0))], 9: [(7, lambda: z_rows(1))],
                               13: [(7, lambda: z_rows(2))]})
            gated(0, GPD_N, GPD_T, None, 12, 8, {1: [(7, lambda: z_rows(3))]})
            with pe.Fori(1, 4) as it:
                gated(it, GPD_N, GPD_T, None, None, 8)

            def sum_squares(count):
                pe.wait_ge(sq2_used, count - 1)
                for m in range(2):
                    pe.matmul(AX[0][:, 0:N], ones[:], SQA[:, m * N:(m + 1) * N], start=m == 0, stop=False)
                pe.wait_ge(sq2_ready, count)
                for m in range(2):
                    ins = pe.matmul(AX[0][:, 0:N], ones[:], GS[:, m * N:(m + 1) * N], start=False, stop=m == 1)
                ins.then_inc(sq2_used, 1)

            def out(it):
                for s in range(2):
                    strip(OUT_N, 8, OUT_T, 4, it, 4 * s, 2 * s, MH, ML,
                          waits=(lambda i: (mlo_ready, 2 * (i + 1))) if isinstance(it, int) and s == 0 else None)

            out(0)
            with pe.Fori(1, 4) as it:
                out(it)

            def mlp(it, between):
                for s in range(4):
                    strip(MLP_N, 32, MLP_T, 24, it, 4 * s, 2 * s, XH, XL, between=between,
                          waits=(lambda i: (xg2_ready, 2 * (i + 1))) if isinstance(it, int) and it + s == 0 else None)
                for j in range(16):
                    d, half = j // 4 * 2 + j % 2, j // 2 % 2
                    tile(MLP_N, 32, MLP_T, 24, it, 16 + j, 8 + 2 * d, 4 * half, 8, OH, OL,
                         (hm_ready, it * 4 + 2 * (half + 1)) if j in (0, 2) else None)

            mlp(0, {3: [(7, lambda: sum_squares(8))]})
            with pe.Fori(1, 7) as it:
                mlp(it, {})
            mlp(7, {})
            sum_squares(16)


LINKS = {"qkv": 6, "lru": 8, "gpl": 4, "gpp": 6, "rglru": 1, "mlp": 4}


def kernel(x_prompt, x_sample, state_lru_h, state_lru_conv, state_dn_s, state_dn_conv, state_pool,
           norm_mix, w_in, lru_conv_w, lru_conv_b, lru_gate_a_w, lru_gate_a_b, lru_gate_x_w, lru_gate_x_b,
           lru_lambda, dn_conv_w, dn_a_log, dn_dt_bias, dn_norm_w, pool_w, pool_scale,
           w_br_lru, w_br_dn, w_br_pool, w_out, norm_mlp, w_up, w_down, norm_final):
    import concourse.bacc as bacc
    from concourse.bass_utils import run_bass_kernel_spmd

    a = lambda t: np.asarray(t)
    chan = lambda t: np.ascontiguousarray(t.reshape(t.shape[0], -1, P).transpose(2, 1, 0)).reshape(P, -1)
    vec = lambda t: a(t).reshape(-1, P).T
    head_rows = lambda t: np.pad(a(t).reshape(-1, 1), ((HEADS, P - 2 * HEADS), (0, 0)))
    x = np.concatenate([a(x_prompt).reshape(NP, D), a(x_sample).reshape(NS, D)])
    conv_w = np.concatenate([a(dn_conv_w)[0], a(lru_conv_w)[0]], axis=1)
    conv_in = np.concatenate([a(state_dn_conv)[0], a(state_lru_conv)[0]], axis=2).reshape(DB * (CW - 1), -1)
    params = np.concatenate([vec(norm_mix), vec(norm_mlp), vec(norm_final), chan(conv_w), vec(lru_conv_b),
                             vec(lru_gate_a_b), vec(lru_gate_x_b), vec(lru_lambda), vec(pool_scale),
                             vec(dn_norm_w), head_rows(dn_a_log), head_rows(dn_dt_bias)], axis=1)
    gates = np.zeros((P, KW, 2, P), np.float32)
    for g, t in enumerate((lru_gate_a_w, lru_gate_x_w)):
        t = a(t)[0].reshape(KW, 2, 64, 64)
        for i in range(2):
            gates[64 * i:64 * (i + 1), :, g, 64 * i:64 * (i + 1)] = t[:, i].transpose(1, 0, 2)
    inputs = {
        "x": chan(x), "params": params, "gates": gates.reshape(P, -1), "conv_in": chan(conv_in),
        "lru_h0": chan(a(state_lru_h)[0]), "pool_in": chan(a(state_pool)[0].reshape(DB * PB, W)),
        "pool_w": a(pool_w)[0].reshape(GROUPS, 2, P, GW_).transpose(2, 0, 1, 3).reshape(P, -1),
        "s_in": a(state_dn_s)[0], "w_in": a(w_in)[0],
        "w_back": np.concatenate([a(w_out)[0], a(w_br_lru)[0], a(w_br_dn)[0], a(w_br_pool)[0]]),
        "w_up": a(w_up)[0], "w_down": a(w_down)[0],
    }
    inputs = {k: np.ascontiguousarray(t) for k, t in inputs.items()}
    outputs = {"y": (P, KD * N), "conv_out": (P, CT * 27), "lru_out": (P, KW * (DB + 1)),
               "pool_out": (P, KW * (DB + 1) * PB), "s_out": (DB, HEADS, P, P), "p_out": (HEADS, P, P)}
    nc = bacc.Bacc("TRN2", target_bir_lowering=False, num_devices=1)
    A = {k: nc.dram_tensor("in_" + k, t.shape, F32, kind="ExternalInput").ap() for k, t in inputs.items()}
    A.update({k: nc.dram_tensor("out_" + k, s, F32, kind="ExternalOutput").ap() for k, s in outputs.items()})
    build(nc, A)
    r = run_bass_kernel_spmd(nc, [{"in_" + k: t for k, t in inputs.items()}], core_ids=[0]).results[0]

    rows = lambda k, n: r["out_" + k].reshape(P, -1, n).transpose(2, 1, 0).reshape(n, -1)
    y, conv, lru, pooled = rows("y", N), rows("conv_out", 27), rows("lru_out", 9), rows("pool_out", 135)
    return (y[:NP].reshape(1, NP, D), y[NP:].reshape(DB, DT, D),
            lru[0:1].reshape(1, 1, W), conv[0:3, 3 * W:].reshape(1, 1, 3, W),
            r["out_p_out"].reshape(1, 1, HEADS, P, P), conv[0:3, :3 * W].reshape(1, 1, 3, 3 * W),
            pooled[0:PB].reshape(1, 1, PB, W),
            lru[1:].reshape(1, DB, W), conv[3:, 3 * W:].reshape(1, DB, 3, W),
            r["out_s_out"].reshape(1, DB, HEADS, P, P), conv[3:, :3 * W].reshape(1, DB, 3, 3 * W),
            pooled[PB:].reshape(1, DB, PB, W))
```
